# Optimizing a Trainium2 kernel written in Bass

```python
import math
import jax, jax.numpy as jnp
from jax import lax
import numpy as np

D_MODEL = 1024
BATCH = 1
SEQ = 256
DEPTH = 2

A_HEADS = 8
A_HEAD_DIM = 64
A_ROT_DIM = A_HEAD_DIM // 4
A_WIDTH = A_HEADS * A_HEAD_DIM
MOBA_BLOCK = 256
MOBA_TOPK = 3
MOBA_Q_CHUNK = 16
B_HEADS = 8
B_NOPE_DIM = 64
B_ROPE_DIM = 32
B_QK_DIM = B_NOPE_DIM + B_ROPE_DIM
B_V_DIM = 64
B_WIDTH = B_HEADS * B_V_DIM
B_Q_RANK = 384
B_KV_RANK = 256
ATTN_Q_BLOCK = 128
ROPE_THETA = 500000.0
N_BRANCH = 2
EPS = 1e-6
NEG = -1e30
D_FF = 2816
N_EXPERTS = 8
EXPERT_TOPK = 2
N_DENSE = (DEPTH + 1) // 2
N_MOE = DEPTH // 2

IN_SPLITS = (A_WIDTH, A_WIDTH, A_WIDTH, B_Q_RANK, B_KV_RANK, B_ROPE_DIM, N_BRANCH * D_MODEL)
IN_WIDTH = sum(IN_SPLITS)
SPLIT_IDX = tuple(int(v) for v in np.cumsum(IN_SPLITS)[:-1])

kernel_name = "hybrid_moba_mla_gated_moe_block"

def rms_norm(x, g):
    xf = x.astype(jnp.float32)
    y = xf * lax.rsqrt(jnp.mean(xf * xf, axis=-1, keepdims=True) + EPS)
    return (y * g.astype(jnp.float32)).astype(x.dtype)

def rope_tables(seq, rot_dim):
    inv = ROPE_THETA ** (-jnp.arange(0, rot_dim, 2, dtype=jnp.float32) / rot_dim)
    ang = jnp.arange(seq, dtype=jnp.float32)[:, None] * inv[None, :]
    return jnp.cos(ang), jnp.sin(ang)

def apply_rope(x, cos, sin):
    xf = x.astype(jnp.float32)
    x1, x2 = jnp.split(xf, 2, axis=-1)
    return jnp.concatenate([x1 * cos - x2 * sin, x2 * cos + x1 * sin], axis=-1).astype(x.dtype)

def rope_slice(x, start, rot_dim, cos, sin):
    return jnp.concatenate([x[..., :start],
                            apply_rope(x[..., start:start + rot_dim], cos, sin),
                            x[..., start + rot_dim:]], axis=-1)

def moba_attention(q, k, v):
    b, h, s, dh = q.shape
    nb = -(-s // MOBA_BLOCK)
    pad = nb * MOBA_BLOCK - s
    kp = jnp.pad(k, ((0, 0), (0, 0), (0, pad), (0, 0))).reshape(b, h, nb, MOBA_BLOCK, dh)
    vp = jnp.pad(v, ((0, 0), (0, 0), (0, pad), (0, 0))).reshape(b, h, nb, MOBA_BLOCK, dh)
    k_mean = jnp.mean(kp.astype(jnp.float32), axis=3)
    pos = jnp.arange(s)
    q_blk = pos // MOBA_BLOCK
    gate = jnp.einsum('bhsd,bhnd->bhsn', q.astype(jnp.float32), k_mean)
    past = jnp.arange(nb)[None, :] < q_blk[:, None]
    gate = jnp.where(past, gate, -jnp.inf)
    topk = min(MOBA_TOPK, nb)
    _, sel = lax.top_k(gate, topk)
    own = jnp.broadcast_to(q_blk.astype(sel.dtype), (b, h, s))[..., None]
    sel = jnp.concatenate([sel, own], axis=-1)
    n_slot = topk + 1
    r = jnp.arange(n_slot)
    slot_ok = (r[None, :] == topk) | (r[None, :] < q_blk[:, None])

    base = (jnp.arange(b)[:, None] * h + jnp.arange(h)[None, :]) * nb
    flat_idx = base[:, :, None, None].astype(sel.dtype) + sel
    k_flat = kp.reshape(b * h * nb, MOBA_BLOCK, dh)
    v_flat = vp.reshape(b * h * nb, MOBA_BLOCK, dh)

    nc = s // MOBA_Q_CHUNK
    c = MOBA_Q_CHUNK
    to_chunks = lambda t: t.reshape(b, h, nc, c, *t.shape[3:]).transpose(2, 0, 1, 3, *range(4, t.ndim + 1))
    q_c = to_chunks(q)
    fidx_c = to_chunks(flat_idx)
    sel_c = to_chunks(sel)
    ok_c = slot_ok.reshape(nc, c, n_slot)
    t_c = pos.reshape(nc, c)
    scale = 1.0 / math.sqrt(dh)
    p_off = jnp.arange(MOBA_BLOCK)

    def chunk_fn(args):
        qc, fidx, selc, okc, tc = args
        kg = jnp.take(k_flat, fidx, axis=0)
        vg = jnp.take(v_flat, fidx, axis=0)
        sc = jnp.einsum('bhcd,bhcrpd->bhcrp', qc, kg,
                        preferred_element_type=jnp.float32) * scale
        kpos = selc[..., None] * MOBA_BLOCK + p_off
        valid = okc[None, None, :, :, None] & (kpos <= tc[None, None, :, None, None])
        sc = jnp.where(valid, sc, NEG)
        pr = jax.nn.softmax(sc.reshape(b, h, c, -1), axis=-1).reshape(sc.shape)
        return jnp.einsum('bhcrp,bhcrpd->bhcd', pr.astype(vg.dtype), vg)

    out = lax.map(chunk_fn, (q_c, fidx_c, sel_c, ok_c, t_c))
    return out.transpose(1, 2, 0, 3, 4).reshape(b, h, s, dh)

def causal_attention(q, k, v):
    b, h, s, d = q.shape
    nq = s // ATTN_Q_BLOCK
    q_b = q.reshape(b, h, nq, ATTN_Q_BLOCK, d).transpose(2, 0, 1, 3, 4)
    kpos = jnp.arange(s)
    scale = 1.0 / math.sqrt(d)

    def blk(args):
        qc, i = args
        sc = jnp.einsum('bhqd,bhkd->bhqk', qc, k, preferred_element_type=jnp.float32) * scale
        qpos = i * ATTN_Q_BLOCK + jnp.arange(ATTN_Q_BLOCK)
        sc = jnp.where(kpos[None, :] <= qpos[:, None], sc, NEG)
        pr = jax.nn.softmax(sc, axis=-1)
        return jnp.einsum('bhqk,bhkd->bhqd', pr.astype(v.dtype), v)

    out = lax.map(blk, (q_b, jnp.arange(nq)))
    return out.transpose(1, 2, 0, 3, 4).reshape(b, h, s, -1)

def token_mixer(x, attn_norm, w_in, moba_qn, moba_kn, cq_norm, w_uq, ckv_norm, w_ukv,
                mla_qn, mla_kn, w_br_a, w_br_b, w_out):
    b, s, _ = x.shape
    hn = rms_norm(x, attn_norm)
    proj = hn @ w_in
    qa, ka, va, cq, ckv, kr, gates = jnp.split(proj, SPLIT_IDX, axis=-1)
    heads = lambda t, n: t.reshape(b, s, n, -1).transpose(0, 2, 1, 3)

    cos_a, sin_a = rope_tables(s, A_ROT_DIM)
    qa = rope_slice(rms_norm(heads(qa, A_HEADS), moba_qn), 0, A_ROT_DIM, cos_a, sin_a)
    ka = rope_slice(rms_norm(heads(ka, A_HEADS), moba_kn), 0, A_ROT_DIM, cos_a, sin_a)
    va = heads(va, A_HEADS)
    ya = moba_attention(qa, ka, va)
    ya = ya.transpose(0, 2, 1, 3).reshape(b, s, A_WIDTH)

    cos_b, sin_b = rope_tables(s, B_ROPE_DIM)
    qb = heads(rms_norm(cq, cq_norm) @ w_uq, B_HEADS)
    kv = heads(rms_norm(ckv, ckv_norm) @ w_ukv, B_HEADS)
    k_nope, vb = jnp.split(kv, [B_NOPE_DIM], axis=-1)
    k_rope = jnp.broadcast_to(kr[:, None], (b, B_HEADS, s, B_ROPE_DIM))
    kb = jnp.concatenate([k_nope, k_rope], axis=-1)
    qb = rope_slice(rms_norm(qb, mla_qn), B_NOPE_DIM, B_ROPE_DIM, cos_b, sin_b)
    kb = rope_slice(rms_norm(kb, mla_kn), B_NOPE_DIM, B_ROPE_DIM, cos_b, sin_b)
    yb = causal_attention(qb, kb, vb)
    yb = yb.transpose(0, 2, 1, 3).reshape(b, s, B_WIDTH)

    g_a, g_b = jnp.split(gates, 2, axis=-1)
    merged = jax.nn.sigmoid(g_a) * (ya @ w_br_a) + jax.nn.sigmoid(g_b) * (yb @ w_br_b)
    return merged @ w_out

def swiglu(h, w_gu, w_down):
    g, u = jnp.split(h @ w_gu, 2, axis=-1)
    return (jax.nn.silu(g) * u) @ w_down

def moe_swiglu(h, router_w, w_gu, w_down):
    logits = jnp.einsum('bsd,de->bse', h, router_w, preferred_element_type=jnp.float32)
    top_v, top_i = lax.top_k(logits, EXPERT_TOPK)
    probs = jax.nn.softmax(top_v, axis=-1)
    gate = jnp.einsum('bsk,bske->bse', probs,
                      jax.nn.one_hot(top_i, N_EXPERTS, dtype=jnp.float32))
    y = jnp.zeros_like(h)
    for e in range(N_EXPERTS):
        y = y + gate[..., e:e + 1].astype(h.dtype) * swiglu(h, w_gu[e], w_down[e])
    return y

def setup_inputs(seed: int = 0) -> dict:
    key = jax.random.key(seed)
    ks = jax.random.split(key, 24)
    f32 = jnp.float32

    def w(k, shape, fan_in):
        return jax.random.normal(k, shape, f32) * (fan_in ** -0.5)

    def g(k, shape):
        return 1.0 + 0.1 * jax.random.normal(k, shape, f32)

    return {
        "x": jax.random.normal(ks[0], (BATCH, SEQ, D_MODEL), f32),
        "attn_norm": g(ks[1], (DEPTH, D_MODEL)),
        "w_in": w(ks[2], (DEPTH, D_MODEL, IN_WIDTH), D_MODEL),
        "moba_q_norm": g(ks[3], (DEPTH, A_HEAD_DIM)),
        "moba_k_norm": g(ks[4], (DEPTH, A_HEAD_DIM)),
        "mla_cq_norm": g(ks[5], (DEPTH, B_Q_RANK)),
        "w_uq": w(ks[6], (DEPTH, B_Q_RANK, B_HEADS * B_QK_DIM), B_Q_RANK),
        "mla_ckv_norm": g(ks[7], (DEPTH, B_KV_RANK)),
        "w_ukv": w(ks[8], (DEPTH, B_KV_RANK, B_HEADS * (B_NOPE_DIM + B_V_DIM)), B_KV_RANK),
        "mla_q_norm": g(ks[9], (DEPTH, B_QK_DIM)),
        "mla_k_norm": g(ks[10], (DEPTH, B_QK_DIM)),
        "w_branch_a": w(ks[11], (DEPTH, A_WIDTH, D_MODEL), A_WIDTH),
        "w_branch_b": w(ks[12], (DEPTH, B_WIDTH, D_MODEL), B_WIDTH),
        "w_out": w(ks[13], (DEPTH, D_MODEL, D_MODEL), D_MODEL),
        "ffn_norm": g(ks[14], (DEPTH, D_MODEL)),
        "dense_w_gate_up": w(ks[15], (N_DENSE, D_MODEL, 2 * D_FF), D_MODEL),
        "dense_w_down": w(ks[16], (N_DENSE, D_FF, D_MODEL), D_FF),
        "router_w": w(ks[17], (N_MOE, D_MODEL, N_EXPERTS), D_MODEL),
        "expert_w_gate_up": w(ks[18], (N_MOE, N_EXPERTS, D_MODEL, 2 * D_FF), D_MODEL),
        "expert_w_down": w(ks[19], (N_MOE, N_EXPERTS, D_FF, D_MODEL), D_FF),
    }

def reference(x, attn_norm, w_in, moba_q_norm, moba_k_norm, mla_cq_norm, w_uq, mla_ckv_norm,
              w_ukv, mla_q_norm, mla_k_norm, w_branch_a, w_branch_b, w_out, ffn_norm,
              dense_w_gate_up, dense_w_down, router_w, expert_w_gate_up, expert_w_down):
    for l in range(DEPTH):
        x = x + token_mixer(x, attn_norm[l], w_in[l], moba_q_norm[l], moba_k_norm[l],
                            mla_cq_norm[l], w_uq[l], mla_ckv_norm[l], w_ukv[l],
                            mla_q_norm[l], mla_k_norm[l], w_branch_a[l], w_branch_b[l], w_out[l])
        h = rms_norm(x, ffn_norm[l])
        if l % 2 == 0:
            x = x + swiglu(h, dense_w_gate_up[l // 2], dense_w_down[l // 2])
        else:
            x = x + moe_swiglu(h, router_w[l // 2], expert_w_gate_up[l // 2], expert_w_down[l // 2])
    return x


_drawn_inputs = setup_inputs


def setup_inputs(seed=0):
    import zlib

    import numpy as np

    out = dict(_drawn_inputs(seed))
    spreads = {}
    factors = {}
    for name, (base, spread) in spreads.items():
        noise = np.random.default_rng([zlib.crc32(name.encode()), seed]).standard_normal(out[name].shape)
        drawn = base * np.exp(spread * noise) if base else spread * noise
        out[name] = __import__('jax').numpy.asarray(drawn.astype(out[name].dtype))
    for name, factor in factors.items():
        out[name] = (out[name] * factor).astype(out[name].dtype)
    return out
```

```python
import math
from contextlib import ExitStack

import numpy as np
import concourse.bass as bass
from concourse import mybir

F32 = mybir.dt.float32
I32 = mybir.dt.int32
ALU = mybir.AluOpType
ACT = mybir.ActivationFunctionType
AX_X = mybir.AxisListType.X

P = 128
D = 1024
T = 256
NT = T // P
DT = D // P
DEPTH = 2
EPS = 1e-6
NEG = -1e30
THETA = 500000.0

HEADS = 8
A_DIM, A_ROT = 64, 16
B_NOPE, B_ROT, B_V = 64, 32, 64
B_DIM = B_NOPE + B_ROT
WIDTH = HEADS * A_DIM
Q_RANK, KV_RANK = 384, 256
LOW = Q_RANK + KV_RANK + B_ROT
OFF_Q, OFF_K, OFF_V, OFF_LOW = 0, WIDTH, 2 * WIDTH, 3 * WIDTH
OFF_GATE = OFF_LOW + LOW
DFF = 2816
GROUP = 256
NGROUP = DFF // GROUP
NFT = DFF // P
NEXP, TOPK = 8, 2
CAP = 96
PASSES = -(-T // CAP)
ITEMS = NEXP * PASSES

SLOTS = 4
SLOT = 3 * GROUP * DT

CONST = {}
_at = 0
for _name, _n in (("ident", P), ("mask", 3 * P), ("earlier", P), ("ones", P), ("slot_no", CAP),
                  ("cos_a", NT * A_ROT), ("sin_a", NT * A_ROT), ("cos_b", NT * B_ROT),
                  ("sin_b", NT * B_ROT), ("lower8", NEXP * NEXP)):
    CONST[_name] = (_at, _at + _n)
    _at += _n
NCONST = _at


def constants():
    c = np.zeros((P, NCONST), np.float32)

    def put(name, a):
        c[:, CONST[name][0]:CONST[name][1]] = a

    i = np.arange(P)
    put("ident", np.eye(P))
    diag = np.where(i[None, :] <= i[:, None], 0.0, NEG)
    put("mask", np.concatenate([diag, np.zeros((P, P)), diag], 1))
    put("earlier", i[:, None] < i[None, :])
    put("ones", 1.0)
    put("slot_no", np.arange(CAP)[None, :])
    for name, rot in (("a", A_ROT), ("b", B_ROT)):
        inv = (THETA ** (-np.arange(0, rot, 2, dtype=np.float64) / rot)).astype(np.float32)
        ang = (np.arange(T, dtype=np.float32)[:, None] * inv[None, :]).astype(np.float64)
        cos, sin = np.cos(ang), np.sin(ang)
        both = lambda a, b: np.concatenate([a, b], 1).reshape(NT, P, rot).transpose(1, 0, 2).reshape(P, NT * rot)
        put(f"cos_{name}", both(cos, cos))
        put(f"sin_{name}", both(-sin, sin))
    e = np.arange(NEXP)
    put("lower8", (e[None, :] < e[:, None]).reshape(1, -1))
    return c


class Tile:

    def __init__(self, bank, fill, free, done):
        self.bank, self.fill, self.free, self.done = bank, fill, free, done

    def at(self, i, fills, drains):
        return Tile(self.bank, i * fills + self.fill, i * drains + self.free, i * drains + self.done)


class Banks:

    def __init__(self, n):
        self.fills, self.drains, self.turn = [0] * n, [0] * n, 0

    def use(self, bank, evacs=1):
        t = Tile(bank, self.fills[bank] + 1, self.drains[bank], self.drains[bank] + evacs)
        self.fills[bank] += 1
        self.drains[bank] += evacs
        return t

    def turns(self, n=8, evacs=1):
        self.turn = (self.turn + 1) % n
        return self.use(self.turn, evacs)


class Slots:

    def __init__(self, n):
        self.frees, self.loads = [0] * n, [0] * n
        self.last = [None] * n

    def use(self, slot, dmas, tile_key=None):
        before = self.last[slot]
        self.loads[slot] += 16 * dmas
        if tile_key is None:
            self.frees[slot] += 1
            self.last[slot] = self.frees[slot]
        else:
            self.last[slot] = tile_key
        return slot, before, self.loads[slot]


def trunk(nc, a, out):
    banks, slots = Banks(8), Slots(SLOTS)

    MIX = ["low", "q", "k", "v", "up", "g0", "g1", "g2", "g3", "bra", "brb", "wo0", "wo1"]
    MIX_DMAS = {"up": 2}
    MIX_LAST = {"low": ("ckv", 1), "q": ("q", 1), "k": ("k", 1), "v": ("v", 1), "up": ("ukv", 1, 1),
                "g0": ("gate", 1), "g1": ("gate", 3), "g2": ("gate", 5), "g3": ("gate", 7),
                "bra": ("br", DT - 1), "brb": ("br", DT - 1), "wo0": None, "wo1": ("wo", 1, 1)}
    chunk, tile = {}, {}

    def plan_norm(n):
        for dp in range(DT // 2):
            tile["hT", n, dp] = banks.turns(8, 2)

    def plan_mixer(l):
        for j, name in enumerate(MIX):
            chunk[l, name] = slots.use(
                j % SLOTS, MIX_DMAS.get(name, 1), MIX_LAST[name] and (MIX_LAST[name][0], l, *MIX_LAST[name][1:]))
        plan_norm(2 * l)
        for t in range(NT):
            tile["cq", l, t] = banks.turns()
            tile["ckv", l, t] = banks.turns()
        for name in "qkv":
            for t in range(NT):
                tile[name, l, t] = banks.turns()
        for j, evacs in enumerate((2, 1, 2)):
            tile["lowT", l, j] = banks.turns(8, evacs)
        for t in range(NT):
            for half in range(2):
                tile["uq", l, t, half] = banks.turns()
        for t in range(NT):
            for half in range(2):
                tile["ukv", l, t, half] = banks.turns(8, 2)
        for hp in range(4):
            tile["aT", l, hp] = banks.turns()
        banks.turn = 3
        tile["s", l, 0] = banks.turns(4)
        for k in range(16):
            if k + 1 < 16:
                tile["s", l, k + 1] = banks.turns(4)
            tile["pT", l, k] = banks.turns(4)
            if k % 2 == 0:
                tile["gate", l, k // 2] = banks.use(4 + k // 2 % 2)
            if k in (6, 7):
                for h in range(4 * (k - 6), 4 * (k - 6) + 4):
                    tile["bT", l, h] = banks.turns(4)
            if k % 4 == 0:
                tile["y", l, k // 4] = banks.use(6 + k // 4 % 2)
            if k == 10:
                for j in range(2):
                    tile["yT", l, 0, j] = banks.turns(4)
        for j in range(2):
            tile["yT", l, 1, j] = banks.turns(4)
        for m in range(DT):
            tile["br", l, m] = banks.turns(6)
        for t in range(NT):
            for half in range(2):
                tile["wo", l, t, half] = banks.turns(8)
        plan_norm(2 * l + 1)

    plan_mixer(0)
    DENSE_TURNS = NGROUP // 2
    DENSE_SLOTS = (1, 2)
    dense_chunk = {}
    DENSE_FREES = [slots.frees[s] for s in DENSE_SLOTS]
    for s in range(2):
        dense_chunk[s] = slots.use(DENSE_SLOTS[s], 3)
        for _ in range(DENSE_TURNS - 1):
            slots.use(DENSE_SLOTS[s], 3)
    dense_chunk[2] = slots.use(DENSE_SLOTS[0], 3, ("dense", 1, 1))
    dense_gu = {}
    for s in range(4):
        dense_gu[s] = banks.use(s)
        for _ in range(DENSE_TURNS - 1):
            banks.use(s)
    for s in range(2):
        dense_gu[4 + s] = banks.use(s)
    for t in range(NT):
        for half in range(2):
            tile["dense", t, half] = banks.use(4 + 2 * t + half)
    plan_mixer(1)
    tile["route"] = banks.use(0)
    tile["rank"] = banks.use(1, 1)
    EXP_SLOTS = [(1, 2, 3, 0)[j % 4] for j in range(NGROUP)]
    frees0 = list(slots.frees)
    exp_chunk = [slots.use(s, 3, None if j < NGROUP - 1 else "last") for j, s in enumerate(EXP_SLOTS)]
    EXP_USES = [EXP_SLOTS.count(s) for s in range(SLOTS)]
    EXP_FREES = [x - y for x, y in zip(slots.frees, frees0)]
    exp_tile = {}
    tile["gather0"] = [banks.use(2, 4), banks.use(3, 4)]
    base_fills, base_drains = list(banks.fills), list(banks.drains)
    for ft in range(NFT):
        exp_tile["gu", ft] = banks.use(ft % 2)
    exp_tile["yT", 0], exp_tile["yT", 1] = banks.use(4), banks.use(5)
    exp_tile["y", 0], exp_tile["y", 1] = banks.use(6), banks.use(7)
    exp_tile["selT",] = banks.use(3)
    SCATTER_BANKS = (6, 7, 2, 3)
    for j, b in enumerate(SCATTER_BANKS):
        exp_tile["scatter", j] = banks.use(b)
    exp_tile["gather", 0], exp_tile["gather", 1] = banks.use(2, 4), banks.use(3, 4)
    EXP_FILLS = [x - y for x, y in zip(banks.fills, base_fills)]
    EXP_DRAINS = [x - y for x, y in zip(banks.drains, base_drains)]

    def item_tile(i, *key):
        t = exp_tile[key]
        return t.at(i, EXP_FILLS[t.bank], EXP_DRAINS[t.bank])

    with ExitStack() as ctx:
        def sb(name, shape, dt=F32):
            return ctx.enter_context(nc.sbuf_tensor(name, shape, dt))

        def sem(name):
            return ctx.enter_context(nc.semaphore(name))

        ps = [ctx.enter_context(nc.psum_tensor(f"ps{b}", [P, 512], F32)) for b in range(8)]
        ring = [sb(f"ring{s}", [P, SLOT]) for s in range(SLOTS)]
        x = sb("x_res", [P, NT, D])
        h = sb("h_scaled", [P, NT, D])
        hT = sb("hT", [P, DT, T])
        cst = sb("cst", [P, NCONST])
        gcol_rows = sb("gcol_rows", [2 * (2 * DT + 5), P])
        gcol = sb("gcol", [P, 2 * (2 * DT + 5)])
        g_heads = sb("g_heads", [P, DEPTH, 2 * A_DIM + 2 * B_DIM])
        router = sb("router", [P, DT, NEXP])
        small = sb("small", [P, 212])
        half_neg = sb("half_neg", [P, 16])
        mix = sb("mix", [P, 20224])
        n_items = sb("n_items", [1, 1], I32)

        def con(name):
            return cst[:, CONST[name][0]:CONST[name][1]]

        ident = con("ident")
        ss_x, rs_x = small[:, 0:2], small[:, 2:4]
        ss_low, rs_low = small[:, 4:8], small[:, 8:12]
        neg_max = small[:, 12:16].rearrange("p (b c) -> p b c", b=2)
        row_max = small[:, 16:20].rearrange("p (b c) -> p b c", b=2)
        ss_h = small[:, 20:84].rearrange("p (w c) -> p w c", w=4)
        rs_h = small[:, 84:148].rearrange("p (w c) -> p w c", w=4)
        row_sum = small[:, 148:180].rearrange("p (b t h) -> p b t h", b=2, t=2)
        row_inv = small[:, 180:212].rearrange("p (b t h) -> p b t h", b=2, t=2)

        top = [0]

        def part(n):
            top[0] += n
            return top[0] - n

        o_low = part(2 * NT * WIDTH + 2 * 3 * P)
        low = mix[:, o_low:o_low + NT * LOW].rearrange("p (t c) -> p t c", t=NT)
        lowT = mix[:, o_low + NT * LOW:o_low + NT * LOW + 5 * T].rearrange("p (r c) -> p r c", r=5)
        y = mix[:, o_low:o_low + 2 * NT * WIDTH].rearrange("p (b t c) -> p b t c", b=2, t=NT)
        o_gate = part(2 * DT * T)
        gate = mix[:, o_gate:o_gate + 2 * DT * T].rearrange("p (m c) -> p m c", m=2 * DT)
        sq = [mix[:, o_gate + w * NT * HEADS * B_DIM:o_gate + (w + 1) * NT * HEADS * B_DIM] for w in range(2)]
        o_qka = part(2 * NT * WIDTH)
        qk_a = mix[:, o_qka:o_qka + 2 * NT * WIDTH].rearrange("p (w t c) -> p w t c", w=2, t=NT)
        yT = mix[:, o_qka:o_qka + 8 * T].rearrange("p (m c) -> p m c", m=8)
        o_v = part(2 * NT * WIDTH)
        v = mix[:, o_v:o_v + 2 * NT * WIDTH].rearrange("p (b t c) -> p b t c", b=2, t=NT)
        o_qkb = part(2 * NT * HEADS * B_DIM)
        qk_b = mix[:, o_qkb:o_qkb + 2 * NT * HEADS * B_DIM].rearrange("p (w t c) -> p w t c", w=2, t=NT)
        o_ta = part(4 * 4 * P)
        qkT_a = mix[:, o_ta:o_ta + 4 * 4 * P].rearrange("p (g c) -> p g c", g=4)
        o_tb = part(HEADS * 4 * P)
        qkT_b = mix[:, o_tb:o_tb + HEADS * 4 * P].rearrange("p (g c) -> p g c", g=HEADS)
        merged = mix[:, o_tb:o_tb + DT * T].rearrange("p (m c) -> p m c", m=DT)
        prod = mix[:, o_tb + DT * T:o_tb + DT * T + 4 * T].rearrange("p (b c) -> p b c", b=2)
        hflat = h[:, :, :].rearrange("p t c -> p (t c)")
        sc = hflat[:, 0:768].rearrange("p (b c) -> p b c", b=2)
        pr = hflat[:, 768:1536].rearrange("p (b c) -> p b c", b=2)
        rot_tmp = hflat[:, 1536:2048]
        pT = mix[:, o_low + 2 * NT * WIDTH:o_low + 2 * NT * WIDTH + 2 * 3 * P].rearrange("p (b c) -> p b c", b=2)
        assert top[0] <= 20224, top[0]

        top[0] = 0
        o = part(2 * T)
        sg = mix[:, o:o + 2 * T].rearrange("p (b c) -> p b c", b=2)
        o = part(2 * T)
        hff = mix[:, o:o + 2 * T].rearrange("p (b c) -> p b c", b=2)
        o = part(NT * CAP)
        sel = mix[:, o:o + NT * CAP].rearrange("p (t c) -> p t c", t=NT)
        o = part(NT * CAP)
        selg = mix[:, o:o + NT * CAP].rearrange("p (t c) -> p t c", t=NT)
        o = part(DT * CAP)
        hsel = mix[:, o:o + DT * CAP].rearrange("p (m c) -> p m c", m=DT)
        o = part(DT * CAP)
        yTe = mix[:, o:o + DT * CAP].rearrange("p (m c) -> p m c", m=DT)
        o = part(D)
        ye = mix[0:CAP, o:o + D]
        o = part(T)
        selT = mix[0:CAP, o:o + T]
        o = part(4 * (ITEMS + 2))
        route = mix[:, o:o + 4 * (ITEMS + 2)].rearrange("p (q i) -> p q i", q=4)
        o = part(8)
        stage, stage_g = mix[:, o:o + 4], mix[:, o + 4:o + 8]
        o = part(16 * 8)
        r16 = [mix[:, o + 16 * j:o + 16 * j + 16].rearrange("p (t e) -> p t e", t=NT) for j in range(8)]
        o = part(2 * 128)
        r128 = [mix[:, o + 128 * j:o + 128 * j + 128].rearrange("p (t e j) -> p t e j", t=NT, e=NEXP) for j in range(2)]
        o = part(16)
        r2 = [mix[:, o + 2 * j:o + 2 * j + 2] for j in range(8)]

        loaded = [sem(f"slot{s}_loaded") for s in range(SLOTS)]
        freed = [sem(f"slot{s}_freed") for s in range(SLOTS)]
        filled = [sem(f"bank{b}_filled") for b in range(8)]
        drained = [sem(f"bank{b}_drained") for b in range(8)]
        x_in = sem("x_in")
        const_in = sem("const_in")
        gain_in = sem("gain_in")
        half_set = sem("half_set")
        gcol_set = sem("gcol_set")
        norm_sq = sem("norm_sq")
        norm_ms = sem("norm_ms")
        norm_rstd = sem("norm_rstd")
        h_scaled = sem("h_scaled")
        low_sq = sem("low_sq")
        low_ms = sem("low_ms")
        low_rstd = sem("low_rstd")
        low_scaled = sem("low_scaled")
        kr_placed = sem("kr_placed")
        kb_copied = sem("kb_copied")
        sq_ready = sem("sq_ready")
        sq_used = sem("sq_used")
        head_ms = sem("head_ms")
        head_rstd = sem("head_rstd")
        qk_normed = sem("qk_normed")
        max_ready = sem("max_ready")
        exp_done = sem("exp_done")
        pv_done = sem("pv_done")
        gate_copied = sem("gate_copied")
        gate_ready = sem("gate_ready")
        merged_ready = sem("merged_ready")
        silu_done = sem("silu_done")
        route_in = sem("route_in")
        route_exp = sem("route_exp")
        sel_bits = sem("sel_bits")
        route_ready = sem("route_ready")
        items_known = sem("items_known")
        moe_zeroed = sem("moe_zeroed")
        sel_ready = sem("sel_ready")
        selg_ready = sem("selg_ready")
        staged = sem("staged")
        dve_step = sem("dve_step")
        out_done = sem("out_done")

        def view(b, *shape):
            n = math.prod(shape)
            flat = ps[b][:, 0:n]
            return flat if len(shape) == 1 else flat.rearrange("p (a c) -> p a c", a=shape[0])

        def w_view(slot, kts, cols, at=0):
            return ring[slot][:, at:at + kts * cols].rearrange("p (k c) -> p k c", k=kts)

        GU = DT * GROUP

        def ffn_views(slot):
            return (w_view(slot, DT, GROUP), w_view(slot, DT, GROUP, GU), w_view(slot, GROUP // P, D, 2 * GU))

        G0 = {"attn": 0, "ffn": DT, "cq": 2 * DT, "ckv": 2 * DT + 3}
        GL = 2 * DT + 5

        def gain(l, name, j):
            c = l * GL + G0[name] + j
            return gcol[:, c:c + 1]

        GAIN_ROW_DMAS = 4 * DEPTH

        block = ctx.enter_context(nc.Block())

        @block.sync
        def _(sp):
            def rows(ap):
                return ap.rearrange("(k p) c -> p k c", p=P)

            def until_free(slot, before):
                if isinstance(before, int):
                    sp.wait_ge(freed[slot], before)
                elif before is not None:
                    sp.wait_ge(filled[tile[before].bank], tile[before].fill)

            def load_mixer(l, names):
                w_in = a["w_in"][l]
                for name in names:
                    slot, before, _ = chunk[l, name]
                    until_free(slot, before)
                    if name == "up":
                        n = 3 * HEADS * B_DIM
                        parts = [(w_view(slot, 3, HEADS * B_DIM), rows(a["w_uq"][l])),
                                 (w_view(slot, 2, D, n), rows(a["w_ukv"][l]))]
                    elif name[:2] == "br":
                        w = a["w_branch_a"] if name == "bra" else a["w_branch_b"]
                        parts = [(w_view(slot, 4, D), rows(w[l]))]
                    elif name[:2] == "wo":
                        j = int(name[2])
                        parts = [(w_view(slot, 4, D), rows(a["w_out"][l, j * WIDTH:(j + 1) * WIDTH, :]))]
                    else:
                        at, n = {"low": (OFF_LOW, LOW), "q": (OFF_Q, WIDTH), "k": (OFF_K, WIDTH),
                                 "v": (OFF_V, WIDTH)}.get(name) or (OFF_GATE + WIDTH * int(name[1]), WIDTH)
                        parts = [(w_view(slot, DT, n), rows(w_in[:, at:at + n]))]
                    for dst, src in parts:
                        sp.dma_start(dst, src).then_inc(loaded[slot], 16)

            def load_group(slot, gate_up, down, j):
                for dst, src in zip(ffn_views(slot), (gate_up[:, bass.ds(j, GROUP)], gate_up[:, bass.ds(j + DFF, GROUP)],
                                                      down[bass.ds(j, GROUP), :])):
                    sp.dma_start(dst, rows(src)).then_inc(loaded[slot], 16)

            sp.dma_start(x[:, :, :], a["x"][0].rearrange("(t p) c -> p t c", p=P)).then_inc(x_in, 16)
            load_mixer(0, MIX)
            gu, dn = a["dense_w_gate_up"][0], a["dense_w_down"][0]
            for s in range(2):
                slot, before, _ = dense_chunk[s]
                until_free(slot, before)
                load_group(slot, gu, dn, s * GROUP)
            with sp.Fori(1, DENSE_TURNS) as i:
                for s in range(2):
                    slot = dense_chunk[s][0]
                    sp.wait_ge(freed[slot], i + DENSE_FREES[s])
                    load_group(slot, gu, dn, (2 * i + s) * GROUP)
            slot, before, _ = dense_chunk[2]
            until_free(slot, before)
            load_group(slot, gu, dn, (NGROUP - 1) * GROUP)
            load_mixer(1, MIX)

            def load_experts(k):
                with sp.Fori(0 if k else 1, NEXP) as e:
                    load_expert(e, e + k * NEXP)

            def load_expert(e, item):
                gu, dn = a["expert_w_gate_up"][0, e], a["expert_w_down"][0, e]
                frees = [0] * SLOTS
                for j in range(NGROUP):
                    slot, before, _ = exp_chunk[j]
                    if isinstance(item, int) and j < SLOTS:
                        until_free(slot, before)
                    elif j < SLOTS and slot == EXP_SLOTS[-1]:
                        t_ = item_tile(item - 1, "yT", 1)
                        sp.wait_ge(filled[t_.bank], t_.fill)
                    else:
                        sp.wait_ge(freed[slot], item * EXP_FREES[slot] + (frees0[slot] + frees[slot]))
                    frees[slot] += 1
                    load_group(slot, gu, dn, j * GROUP)

            load_expert(0, 0)
            load_experts(0)
            sp.wait_ge(items_known, 1)
            n = sp.value_load(n_items[0:1, 0:1], min_val=NEXP, max_val=ITEMS)
            with sp.If(n > NEXP):
                for k in range(1, PASSES):
                    load_experts(k)
            last = item_tile(n, "scatter", len(SCATTER_BANKS) - 1)
            sp.wait_ge(drained[last.bank], last.done)
            sp.dma_start(out[0].rearrange("(t p) c -> p t c", p=P), x[:, :, :]).then_inc(out_done, 16)
            sp.wait_ge(out_done, 16)

        @block.tensor
        def _(pe):
            def fill(t):
                pe.wait_ge(drained[t.bank], t.free)

            def start(t):
                if t.free:
                    fill(t)

            def evacuated(t):
                pe.wait_ge(drained[t.bank], t.done)

            def arrived(c):
                pe.wait_ge(loaded[c[0]], c[2])

            def norm_transposes(n):
                pe.wait_ge(h_scaled, 2 * n + 2)
                for dp in range(DT // 2):
                    t_ = tile["hT", n, dp]
                    start(t_)
                    for j in range(2):
                        for t in range(NT):
                            last = pe.transpose(ps[t_.bank][:, (2 * j + t) * P:(2 * j + t + 1) * P],
                                                h[:, t, (2 * dp + j) * P:(2 * dp + j + 1) * P], ident)
                    last.then_inc(filled[t_.bank], 1)

            def hT_ready(n):
                for dp in range(DT // 2):
                    evacuated(tile["hT", n, dp])

            def by_tokens(t_, t, w, cols, src, k0=0, kn=DT, first=True, final=True):
                for k in range(kn):
                    last = pe.matmul(ps[t_.bank][:, cols[0]:cols[1]], src[:, k0 + k, t * P:(t + 1) * P], w[k],
                                     start=first and k == 0, stop=final and k == kn - 1)
                return last

            def mixer(l):
                norm_transposes(2 * l)
                hT_ready(2 * l)
                c = chunk[l, "low"]
                arrived(c)
                w = w_view(c[0], DT, LOW)
                for t in range(NT):
                    for name, lo, hi in (("cq", 0, Q_RANK), ("ckv", Q_RANK, LOW)):
                        t_ = tile[name, l, t]
                        start(t_)
                        last = by_tokens(t_, t, [w[:, k, lo:hi] for k in range(DT)], (0, hi - lo), hT)
                        last.then_inc(filled[t_.bank], 1)
                for name in "qkv":
                    c = chunk[l, name]
                    arrived(c)
                    w = w_view(c[0], DT, WIDTH)
                    for t in range(NT):
                        t_ = tile[name, l, t]
                        start(t_)
                        last = by_tokens(t_, t, [w[:, k, :] for k in range(DT)], (0, WIDTH), hT)
                        last.then_inc(filled[t_.bank], 1)
                pe.wait_ge(low_scaled, 4 * (l + 1))
                for j, rs in enumerate(((0, 1), (2,), (3, 4))):
                    t_ = tile["lowT", l, j]
                    start(t_)
                    for n, r in enumerate(rs):
                        for t in range(NT):
                            last = pe.transpose(ps[t_.bank][:, (2 * n + t) * P:(2 * n + t + 1) * P],
                                                low[:, t, r * P:(r + 1) * P], ident)
                    last.then_inc(filled[t_.bank], 1)
                for j in range(3):
                    evacuated(tile["lowT", l, j])
                c = chunk[l, "up"]
                arrived(c)
                wq = w_view(c[0], 3, HEADS * B_DIM)
                wkv = w_view(c[0], 2, D, 3 * HEADS * B_DIM)
                for name, w, k0, kn, n in (("uq", wq, 0, 3, HEADS * B_DIM // 2), ("ukv", wkv, 3, 2, D // 2)):
                    for t in range(NT):
                        for half in range(2):
                            t_ = tile[name, l, t, half]
                            start(t_)
                            last = by_tokens(t_, t, [w[:, k, half * n:(half + 1) * n] for k in range(kn)], (0, n),
                                             lowT, k0, kn)
                            last.then_inc(filled[t_.bank], 1)
                pe.wait_ge(qk_normed, 4 * l + 2)
                for hp in range(4):
                    t_ = tile["aT", l, hp]
                    start(t_)
                    for w in range(2):
                        for t in range(NT):
                            last = pe.transpose(ps[t_.bank][:, (2 * w + t) * P:(2 * w + t + 1) * P],
                                                qk_a[:, w, t, hp * P:(hp + 1) * P], ident)
                    last.then_inc(filled[t_.bank], 1)

                def q_k(k):
                    if k < HEADS:
                        lo = (k % 2) * A_DIM
                        both = qkT_a[lo:lo + A_DIM, k // 2, :]
                    else:
                        both = qkT_b[0:B_DIM, k - HEADS, :]
                    return both[:, 0:T], both[:, T:2 * T]

                def scores(k):
                    evacuated(tile["aT", l, k // 2] if k < HEADS else tile["bT", l, k - HEADS])
                    t_ = tile["s", l, k]
                    start(t_)
                    q, key = q_k(k)
                    pe.matmul(ps[t_.bank][:, 0:P], q[:, 0:P], key[:, 0:P], start=True, stop=True)
                    pe.matmul(ps[t_.bank][:, P:3 * P], q[:, P:T], key, start=True, stop=True).then_inc(filled[t_.bank], 1)

                def turn_probs(k):
                    pe.wait_ge(exp_done, 16 * l + k + 1)
                    t_ = tile["pT", l, k]
                    start(t_)
                    for j in range(3):
                        last = pe.transpose(ps[t_.bank][:, j * P:(j + 1) * P], pr[:, k % 2, j * P:(j + 1) * P], ident)
                    last.then_inc(filled[t_.bank], 1)

                def gates(k):
                    t_ = tile["gate", l, k // 2]
                    c = chunk[l, f"g{k // 4}"]
                    if k % 2 == 0:
                        start(t_)
                    if k % 4 == 0:
                        arrived(c)
                    w = w_view(c[0], DT, WIDTH)
                    for kt in range(DT):
                        last = pe.matmul(ps[t_.bank][:, (k % 2) * T:(k % 2 + 1) * T], w[:, kt, (k % 4) * P:(k % 4 + 1) * P],
                                         hT[:, kt, :], start=kt == 0, stop=kt == DT - 1)
                    if k % 2:
                        last.then_inc(filled[t_.bank], 1)

                def turn_b(hd):
                    pe.wait_ge(qk_normed, 4 * l + 4)
                    t_ = tile["bT", l, hd]
                    start(t_)
                    for w in range(2):
                        for t in range(NT):
                            last = pe.transpose(ps[t_.bank][0:B_DIM, (2 * w + t) * P:(2 * w + t + 1) * P],
                                                qk_b[:, w, t, hd * B_DIM:(hd + 1) * B_DIM], ident)
                    last.then_inc(filled[t_.bank], 1)

                def values(k):
                    t_ = tile["y", l, k // 4]
                    evacuated(tile["pT", l, k])
                    if k % 4 == 0:
                        start(t_)
                    if k == 0:
                        for t in range(NT):
                            evacuated(tile["v", l, t])
                    if k == HEADS:
                        for t in range(NT):
                            for half in range(2):
                                evacuated(tile["ukv", l, t, half])
                    vv = v[:, k // HEADS, :, (k % HEADS) * A_DIM:(k % HEADS + 1) * A_DIM]
                    o0 = (k % 4) * A_DIM
                    o1 = T + o0
                    bank = ps[t_.bank]
                    pe.matmul(bank[:, o0:o0 + A_DIM], pT[:, k % 2, 0:P], vv[:, 0, :], start=True, stop=True)
                    pe.matmul(bank[:, o1:o1 + A_DIM], pT[:, k % 2, P:2 * P], vv[:, 0, :], start=True, stop=False)
                    last = pe.matmul(bank[:, o1:o1 + A_DIM], pT[:, k % 2, 2 * P:3 * P], vv[:, 1, :], start=False, stop=True)
                    if k % 4 == 3:
                        last.then_inc(filled[t_.bank], 1)
                    else:
                        last.then_inc(pv_done, 1)

                def turn_y(b):
                    for quad in range(2):
                        evacuated(tile["y", l, 2 * b + quad])
                    for j in range(2):
                        t_ = tile["yT", l, b, j]
                        start(t_)
                        for m in range(2):
                            for t in range(NT):
                                last = pe.transpose(ps[t_.bank][:, (2 * m + t) * P:(2 * m + t + 1) * P],
                                                    y[:, b, t, (2 * j + m) * P:(2 * j + m + 1) * P], ident)
                        last.then_inc(filled[t_.bank], 1)

                scores(0)
                for k in range(16):
                    if k + 1 < 16:
                        scores(k + 1)
                    turn_probs(k)
                    gates(k)
                    if k in (6, 7):
                        for hd in range(4 * (k - 6), 4 * (k - 6) + 4):
                            turn_b(hd)
                    values(k)
                    if k == 10:
                        turn_y(0)
                turn_y(1)
                wb = []
                for name in ("bra", "brb"):
                    c = chunk[l, name]
                    arrived(c)
                    wb.append(w_view(c[0], 4, D))
                for b in range(2):
                    for j in range(2):
                        evacuated(tile["yT", l, b, j])
                for m in range(DT):
                    t_ = tile["br", l, m]
                    start(t_)
                    for b in range(2):
                        for kt in range(4):
                            last = pe.matmul(ps[t_.bank][:, b * T:(b + 1) * T], wb[b][:, kt, m * P:(m + 1) * P],
                                             yT[:, 4 * b + kt, :], start=kt == 0, stop=kt == 3)
                    last.then_inc(filled[t_.bank], 1)
                for j in range(2):
                    c = chunk[l, f"wo{j}"]
                    arrived(c)
                    w = w_view(c[0], 4, D)
                    for kk in range(4):
                        kt = 4 * j + kk
                        pe.wait_ge(merged_ready, DT * l + kt + 1)
                        for t in range(NT):
                            for half in range(2):
                                t_ = tile["wo", l, t, half]
                                if kt == 0:
                                    start(t_)
                                last = pe.matmul(ps[t_.bank][:, :], merged[:, kt, t * P:(t + 1) * P],
                                                 w[:, kk, half * 512:(half + 1) * 512], start=kt == 0, stop=kt == DT - 1)
                                if kt == DT - 1:
                                    last.then_inc(filled[t_.bank], 1)
                    if j == 0:
                        last.then_inc(freed[c[0]], 1)
                norm_transposes(2 * l + 1)
                hT_ready(2 * l + 1)

            def ffn_in(bank, wg, wu, s, src, n):
                for j, w in enumerate((wg, wu)):
                    for kt in range(DT):
                        last = pe.matmul(ps[bank][:, j * n:(j + 1) * n], w[:, kt, s * P:(s + 1) * P], src[:, kt, 0:n],
                                         start=kt == 0, stop=kt == DT - 1)
                return last

            def dense():
                def gate_up(t_, slot, s):
                    fill(t_)
                    wg, wu, _ = ffn_views(slot)
                    ffn_in(t_.bank, wg, wu, s, hT, T).then_inc(filled[t_.bank], 1)

                def down(t_, slot, s, ft, final=False):
                    evacuated(t_)
                    wd = ffn_views(slot)[2]
                    for t in range(NT):
                        for half in range(2):
                            o = tile["dense", t, half]
                            last = pe.matmul(ps[o.bank][:, :], hff[:, ft % 2, t * P:(t + 1) * P],
                                             wd[:, s, half * 512:(half + 1) * 512], start=False, stop=final,
                                             skip_group_check=True)
                            if final:
                                last.then_inc(filled[o.bank], 1)
                    return last

                def down_first(t_, slot):
                    evacuated(t_)
                    wd = ffn_views(slot)[2]
                    for t in range(NT):
                        for half in range(2):
                            o = tile["dense", t, half]
                            fill(o)
                            pe.matmul(ps[o.bank][:, :], hff[:, 0, t * P:(t + 1) * P],
                                      wd[:, 0, half * 512:(half + 1) * 512], start=True, stop=False,
                                      skip_group_check=True)

                def turn(i, first):
                    for q in range(4):
                        s_next = (q + 1) % 4
                        g = s_next // 2
                        turn_next = i + 1 if q == 3 else i
                        t_next = dense_gu[s_next].at(turn_next, 1, 1)
                        slot, _, full = dense_chunk[g]
                        if s_next % 2 == 0:
                            pe.wait_ge(loaded[slot], turn_next * 48 + full)
                        gate_up(t_next, slot, s_next % 2)
                        now = dense_gu[q].at(i, 1, 1)
                        slot = dense_chunk[q // 2][0]
                        if first and q == 0:
                            down_first(now, slot)
                        else:
                            last = down(now, slot, q % 2, q)
                        if q % 2:
                            last.then_inc(freed[slot], 1)

                slot, _, full = dense_chunk[0]
                pe.wait_ge(loaded[slot], full)
                gate_up(dense_gu[0], slot, 0)
                turn(0, True)
                with pe.Fori(1, DENSE_TURNS) as i:
                    turn(i, False)
                slot = dense_chunk[2][0]
                gate_up(dense_gu[5], slot, 1)
                down(dense_gu[4], slot, 0, 0)
                down(dense_gu[5], slot, 1, 1, True)

            def routing():
                t_ = tile["route"]
                start(t_)
                for t in range(NT):
                    for kt in range(DT):
                        last = pe.matmul(ps[t_.bank][:, t * NEXP:(t + 1) * NEXP], hT[:, kt, t * P:(t + 1) * P],
                                         router[:, kt, :], start=kt == 0, stop=kt == DT - 1)
                last.then_inc(filled[t_.bank], 1)
                pe.wait_ge(sel_bits, 1)
                t_ = tile["rank"]
                start(t_)
                chosen = r16[3]
                before, every = con("earlier"), con("ones")
                bank = ps[t_.bank]
                pe.matmul(bank[:, 0:8], before, chosen[:, 0, :], start=True, stop=True)
                pe.matmul(bank[:, 8:16], every, chosen[:, 0, :], start=True, stop=False)
                pe.matmul(bank[:, 8:16], before, chosen[:, 1, :], start=False, stop=True)
                pe.matmul(bank[:, 16:24], every, chosen[:, 0, :], start=True, stop=False)
                pe.matmul(bank[:, 16:24], every, chosen[:, 1, :], start=False, stop=True).then_inc(filled[t_.bank], 1)

            def gather(n_sel, tiles):
                pe.wait_ge(sel_ready, n_sel)
                for g, t_ in enumerate(tiles):
                    fill(t_)
                    for j in range(4):
                        for t in range(NT):
                            last = pe.matmul(ps[t_.bank][:, j * CAP:(j + 1) * CAP],
                                             h[:, t, (4 * g + j) * P:(4 * g + j + 1) * P], sel[:, t, :],
                                             start=t == 0, stop=t == NT - 1)
                    last.then_inc(filled[t_.bank], 1)

            def turn_results(i):
                for j in range(2):
                    evacuated(item_tile(i - 1, "yT", j))
                for j in range(2):
                    t_ = item_tile(i, "y", j)
                    fill(t_)
                    for m in range(4):
                        last = pe.transpose(ps[t_.bank][0:CAP, m * P:(m + 1) * P], yTe[:, 4 * j + m, :], ident)
                    last.then_inc(filled[t_.bank], 1)
                pe.wait_ge(selg_ready, i + 1)
                t_ = item_tile(i, "selT")
                fill(t_)
                for t in range(NT):
                    last = pe.transpose(ps[t_.bank][0:CAP, t * P:(t + 1) * P], selg[:, t, :], ident)
                last.then_inc(filled[t_.bank], 1)

            def scatter(i):
                for key in (("y", 0), ("y", 1), ("selT",)):
                    evacuated(item_tile(i, *key))
                for t in range(NT):
                    for half in range(2):
                        t_ = item_tile(i, "scatter", 2 * t + half)
                        fill(t_)
                        pe.matmul(ps[t_.bank][:, :], selT[:, t * P:(t + 1) * P], ye[:, half * 512:(half + 1) * 512],
                                  start=True, stop=True).then_inc(filled[t_.bank], 1)

            def expert(i):
                def gate_up(ft):
                    slot, _, full = exp_chunk[ft // 2]
                    if ft % 2 == 0:
                        pe.wait_ge(loaded[slot], i * (48 * EXP_USES[slot]) + full)
                    t_ = item_tile(i, "gu", ft)
                    fill(t_)
                    wg, wu, _ = ffn_views(slot)
                    ffn_in(t_.bank, wg, wu, ft % 2, hsel, CAP).then_inc(filled[t_.bank], 1)

                def down(ft):
                    slot = exp_chunk[ft // 2][0]
                    evacuated(item_tile(i, "gu", ft))
                    wd = ffn_views(slot)[2]
                    for m in range(DT):
                        o = item_tile(i, "yT", m // 4)
                        if ft == 0 and m % 4 == 0:
                            fill(o)
                        last = pe.matmul(ps[o.bank][:, (m % 4) * CAP:(m % 4 + 1) * CAP], wd[:, ft % 2, m * P:(m + 1) * P],
                                         hff[:, ft % 2, 0:CAP], start=ft == 0 and m % 4 == 0, stop=ft == NFT - 1,
                                         skip_group_check=True)
                        if ft == NFT - 1 and m % 4 == 3:
                            last.then_inc(filled[o.bank], 1)
                    if ft % 2 and ft < NFT - 1:
                        last.then_inc(freed[slot], 1)

                gate_up(0)
                turn_results(i)
                gate_up(1)
                down(0)
                scatter(i)
                for ft in range(2, NFT):
                    gate_up(ft)
                    down(ft - 1)
                gather(i + 2, [item_tile(i, "gather", g) for g in range(2)])
                down(NFT - 1)
                for g in range(2):
                    evacuated(item_tile(i, "gather", g))

            pe.wait_ge(const_in, 16)
            pe.wait_ge(gain_in, 16 * GAIN_ROW_DMAS)
            pe.transpose(ps[7][:, 0:2 * GL], gcol_rows[:, :], ident[0:2 * GL, 0:2 * GL]).then_inc(gcol_set, 1)
            mixer(0)
            dense()
            mixer(1)
            routing()
            pe.wait_ge(moe_zeroed, 1)
            gather(1, tile["gather0"])
            for g in range(2):
                evacuated(tile["gather0"][g])
            with pe.Fori(0, NEXP) as i:
                expert(i)
            pe.wait_ge(items_known, 1)
            n = pe.value_load(n_items[0:1, 0:1], min_val=NEXP, max_val=ITEMS)
            with pe.If(n > NEXP):
                with pe.Fori(NEXP, ITEMS) as i:
                    expert(i)
            turn_results(n)
            scatter(n)

        @block.scalar
        def _(act):
            def full(t_):
                act.wait_ge(filled[t_.bank], t_.fill)

            act.dma_start(cst[:, :], a["consts"]).then_inc(const_in, 16)
            for l in range(DEPTH):
                for name, w, n in (("attn", "attn_norm", DT), ("ffn", "ffn_norm", DT), ("cq", "mla_cq_norm", 3),
                                   ("ckv", "mla_ckv_norm", 2)):
                    r = l * GL + G0[name]
                    act.dma_start(gcol_rows[r:r + n, :], a[w][l].rearrange("(r c) -> r c", c=P)).then_inc(gain_in, 16)
                at = 0
                for w, n in (("moba_q_norm", A_DIM), ("moba_k_norm", A_DIM), ("mla_q_norm", B_DIM), ("mla_k_norm", B_DIM)):
                    act.dma_start(g_heads[:, l, at:at + n], a[w][l].partition_broadcast(P)).then_inc(route_in, 16)
                    at += n
            act.dma_start(router[:, :, :], a["router_w"][0].rearrange("(k p) e -> p k e", p=P)).then_inc(route_in, 16)

            def copy_out(dst, t_, src):
                act.copy(dst, src).then_inc(drained[t_.bank], 1)

            def norm(n, l, gain_name):
                for t in range(NT):
                    act.activation(h[:, t, :], x[:, t, :], ACT.Square, accum_out=ss_x[:, t:t + 1]).then_inc(norm_sq, 1)
                for dp in range(1, DT // 2, 2):
                    t_ = tile["hT", n, dp]
                    full(t_)
                    for j in range(2):
                        act.mul(hT[:, 2 * dp + j, :], view(t_.bank, 2, T)[:, j, :],
                                gain(l, gain_name, 2 * dp + j)).then_inc(drained[t_.bank], 1)

            def mixer(l):
                norm(2 * l, l, "attn")
                for t in range(NT):
                    for name, j, n, at in (("cq", 0, Q_RANK, 0), ("ckv", 1, KV_RANK, Q_RANK)):
                        t_ = tile[name, l, t]
                        full(t_)
                        c = 2 * t + j
                        act.activation(mix[:, o_gate + c * Q_RANK:o_gate + c * Q_RANK + n], ps[t_.bank][:, 0:n], ACT.Square,
                                       accum_out=ss_low[:, c:c + 1]).then_inc(low_sq, 1)
                        m = n if name == "cq" else LOW - Q_RANK
                        copy_out(low[:, t, at:at + m], t_, ps[t_.bank][:, 0:m])
                act.wait_ge(low_sq, 4 * (l + 1))
                for w, name in enumerate("qk"):
                    for t in range(NT):
                        t_ = tile[name, l, t]
                        full(t_)
                        last = act.activation(sq[w][:, t * WIDTH:(t + 1) * WIDTH], ps[t_.bank][:, :], ACT.Square)
                        if t == NT - 1:
                            last.then_inc(sq_ready, 1)
                        copy_out(qk_a[:, w, t, :], t_, ps[t_.bank][:, :])
                for t in range(NT):
                    t_ = tile["v", l, t]
                    full(t_)
                    copy_out(v[:, 0, t, :], t_, ps[t_.bank][:, :])
                for j, rs in enumerate(((0, 1), (2,), (3, 4))):
                    t_ = tile["lowT", l, j]
                    full(t_)
                    for n, r in enumerate(rs):
                        g = gain(l, "cq", r) if r < 3 else gain(l, "ckv", r - 3)
                        act.mul(lowT[:, r, :], ps[t_.bank][:, n * T:(n + 1) * T], g).then_inc(drained[t_.bank], 1)
                act.wait_ge(sq_used, 4 * l + 1)
                n = HEADS * B_DIM // 2
                for t in range(NT):
                    for half in range(2):
                        t_ = tile["uq", l, t, half]
                        full(t_)
                        at = (2 * t + half) * n
                        last = act.activation(sq[0][:, at:at + n], ps[t_.bank][:, 0:n], ACT.Square)
                        if t + half == 2:
                            last.then_inc(sq_ready, 1)
                        copy_out(qk_b[:, 0, t, half * n:(half + 1) * n], t_, ps[t_.bank][:, 0:n])
                for t in range(NT):
                    for half in range(2):
                        t_ = tile["ukv", l, t, half]
                        full(t_)
                        src = ps[t_.bank][:, :].rearrange("p (h c) -> p h c", h=4)
                        dst = qk_b[:, 1, t, half * n:(half + 1) * n].rearrange("p (h c) -> p h c", h=4)
                        copy_out(dst[:, :, 0:B_NOPE], t_, src[:, :, 0:B_NOPE])
                        copy_out(v[:, 1, t, half * 4 * B_V:(half + 1) * 4 * B_V].rearrange("p (h c) -> p h c", h=4), t_,
                                 src[:, :, B_NOPE:])
                act.wait_ge(kr_placed, l + 1)
                for t in range(NT):
                    for half in range(2):
                        t_ = tile["ukv", l, t, half]
                        act.wait_ge(drained[t_.bank], t_.done)
                act.wait_ge(sq_used, 4 * l + 2)
                for t in range(NT):
                    last = act.activation(sq[1][:, t * 2 * n:(t + 1) * 2 * n], qk_b[:, 1, t, :], ACT.Square)
                last.then_inc(sq_ready, 1)
                for hp in range(4):
                    t_ = tile["aT", l, hp]
                    full(t_)
                    copy_out(qkT_a[:, hp, :], t_, ps[t_.bank][:, :])

                def exponentials(k):
                    act.wait_ge(max_ready, 16 * l + k + 1)
                    b, hd = k // HEADS, k % HEADS
                    for t, (lo, hi) in enumerate(((0, P), (P, 3 * P))):
                        last = act.activation(pr[:, k % 2, lo:hi], sc[:, k % 2, lo:hi], ACT.Exp,
                                              bias=neg_max[:, k % 2, t:t + 1], accum_out=row_sum[:, b, t, hd:hd + 1])
                    last.then_inc(exp_done, 1)

                exponentials(0)
                for k in range(16):
                    t_ = tile["pT", l, k]
                    full(t_)
                    if k >= 2:
                        used_values(l, k - 2)
                    copy_out(pT[:, k % 2, :], t_, ps[t_.bank][:, 0:3 * P])
                    if k + 1 < 16:
                        exponentials(k + 1)
                    if k % 2:
                        g = k // 2
                        t_ = tile["gate", l, g]
                        full(t_)
                        if g == 0:
                            act.wait_ge(sq_used, 4 * l + 4)
                        copy_out(gate[:, 2 * g:2 * g + 2, :], t_, view(t_.bank, 2, T))
                    if k in (6, 7):
                        for hd in range(4 * (k - 6), 4 * (k - 6) + 4):
                            t_ = tile["bT", l, hd]
                            full(t_)
                            copy_out(qkT_b[0:B_DIM, hd, :], t_, ps[t_.bank][0:B_DIM, :])
                    if k == 10:
                        turned_y(l, 0)
                turned_y(l, 1)
                for g in range(8):
                    t_ = tile["gate", l, g]
                    act.wait_ge(drained[t_.bank], t_.done)
                both = gate.rearrange("p (b m) c -> p b (m c)", b=2)
                for j in range(4):
                    part_ = both[:, :, j * 2 * T:(j + 1) * 2 * T]
                    act.activation(part_, part_, ACT.Sigmoid).then_inc(gate_ready, 1)
                for t in range(NT):
                    for half in range(2):
                        t_ = tile["wo", l, t, half]
                        act.wait_ge(drained[t_.bank], t_.done)
                norm(2 * l + 1, l, "ffn")

            def used_values(l, k):
                if k % 4 == 3:
                    t_ = tile["y", l, k // 4]
                    act.wait_ge(filled[t_.bank], t_.fill)
                else:
                    act.wait_ge(pv_done, 12 * l + k - k // 4 + 1)

            def turned_y(l, b):
                for j in range(2):
                    t_ = tile["yT", l, b, j]
                    full(t_)
                    copy_out(yT[:, 4 * b + 2 * j:4 * b + 2 * j + 2, :], t_, view(t_.bank, 2, T))

            def silu(t_, ft, n):
                full(t_)
                act.activation(sg[:, ft % 2, 0:n], ps[t_.bank][:, 0:n], ACT.Silu).then_inc(silu_done, 1)

            act.wait_ge(x_in, 16)
            act.wait_ge(gain_in, 16 * GAIN_ROW_DMAS)
            act.wait_ge(const_in, 16)
            act.wait_ge(route_in, 16 * 9)
            act.wait_ge(gcol_set, 2)
            mixer(0)
            with act.Fori(0, DENSE_TURNS) as i:
                for s in range(4):
                    silu(dense_gu[s].at(i, 1, 1), s, T)
            for s in range(2):
                silu(dense_gu[4 + s], s, T)
            for t in range(NT):
                for half in range(2):
                    t_ = tile["dense", t, half]
                    act.wait_ge(drained[t_.bank], t_.done)
            mixer(1)
            act.wait_ge(route_ready, 1)
            act.activation(r16[4], r16[1], ACT.Exp).then_inc(route_exp, 1)

            def gathered(t_, g):
                full(t_)
                for j in range(4):
                    m = 4 * g + j
                    act.mul(hsel[:, m, :], ps[t_.bank][:, j * CAP:(j + 1) * CAP], gain(1, "ffn", m)).then_inc(
                        drained[t_.bank], 1)

            gathered(tile["gather0"][1], 1)

            def results(i):
                t_ = item_tile(i, "y", 1)
                full(t_)
                copy_out(ye[:, 512:], t_, ps[t_.bank][0:CAP, :])
                t_ = item_tile(i, "selT")
                full(t_)
                copy_out(selT, t_, ps[t_.bank][0:CAP, 0:T])

            def expert(i):
                silu(item_tile(i, "gu", 0), 0, CAP)
                results(i)
                for ft in range(1, NFT):
                    silu(item_tile(i, "gu", ft), ft, CAP)
                gathered(item_tile(i, "gather", 1), 1)
                t_ = item_tile(i, "yT", 1)
                full(t_)
                copy_out(yTe[:, 4:8, :], t_, view(t_.bank, 4, CAP))

            with act.Fori(0, NEXP) as i:
                expert(i)
            act.wait_ge(items_known, 1)
            n = act.value_load(n_items[0:1, 0:1], min_val=NEXP, max_val=ITEMS)
            with act.If(n > NEXP):
                with act.Fori(NEXP, ITEMS) as i:
                    expert(i)
            results(n)

        @block.vector
        def _(dve):
            steps = [0]

            def step(ins):
                steps[0] += 1
                ins.then_inc(dve_step, 1)
                dve.wait_ge(dve_step, steps[0])

            def full(t_):
                dve.wait_ge(filled[t_.bank], t_.fill)

            def norm(n, l, gain_name):
                dve.wait_ge(norm_rstd, n + 1)
                for t in range(NT):
                    dve.tensor_scalar(h[:, t, :], x[:, t, :], rs_x[:, t:t + 1], None, ALU.mult).then_inc(h_scaled, 1)
                for dp in range(0, DT // 2, 2):
                    t_ = tile["hT", n, dp]
                    full(t_)
                    for j in range(2):
                        dve.tensor_scalar(hT[:, 2 * dp + j, :], view(t_.bank, 2, T)[:, j, :],
                                          gain(l, gain_name, 2 * dp + j), None, ALU.mult).then_inc(drained[t_.bank], 1)

            def head_pieces(l, w):
                branch_b = w >= 2
                buf = (qk_b if branch_b else qk_a)[:, w % 2, :, :]
                dim, rot = (B_DIM, B_ROT) if branch_b else (A_DIM, A_ROT)
                lo = B_NOPE if branch_b else 0
                name = "b" if branch_b else "a"
                heads = buf.rearrange("p t (h c) -> p (t h) c", c=dim)
                g0 = (0, A_DIM, 2 * A_DIM, 2 * A_DIM + B_DIM)[w]
                g = g_heads[:, l, g0:g0 + dim].unsqueeze(1).broadcast_to([P, NT * HEADS, dim])
                rs = rs_h[:, w, :].unsqueeze(2).broadcast_to([P, NT * HEADS, dim])
                by_head = buf.rearrange("p t (h c) -> p t h c", c=dim)
                half = rot // 2
                table = lambda s: con(f"{s}_{name}").rearrange("p (t r) -> p t r", t=NT)
                cos = table("cos").unsqueeze(2).broadcast_to([P, NT, HEADS, rot])
                sin = table("sin").unsqueeze(2).broadcast_to([P, NT, HEADS, rot])
                tmp = rot_tmp[:, 0:NT * HEADS * rot].rearrange("p (t h r) -> p t h r", t=NT, h=HEADS)
                x12 = by_head[:, :, :, lo:lo + rot]

                def scale():
                    dve.wait_ge(head_rstd, 4 * l + w + 1)
                    step(dve.tensor_tensor(heads, heads, rs, ALU.mult))

                def gains():
                    step(dve.tensor_tensor(heads, heads, g, ALU.mult))

                def cross():
                    dve.tensor_tensor(tmp[:, :, :, 0:half], x12[:, :, :, half:], sin[:, :, :, 0:half], ALU.mult)
                    step(dve.tensor_tensor(tmp[:, :, :, half:], x12[:, :, :, 0:half], sin[:, :, :, half:], ALU.mult))

                def straight():
                    step(dve.tensor_tensor(x12, x12, cos, ALU.mult))

                def total():
                    step(dve.tensor_tensor(x12, x12, tmp, ALU.add))
                    dve.sem_inc(qk_normed, 1)

                return [scale, gains, cross, straight, total]

            def mixer(l):
                norm(2 * l, l, "attn")
                dve.wait_ge(low_rstd, l + 1)
                for t in range(NT):
                    for j, (lo, hi) in enumerate(((0, Q_RANK), (Q_RANK, Q_RANK + KV_RANK))):
                        t_ = tile[("cq", "ckv")[j], l, t]
                        dve.wait_ge(drained[t_.bank], t_.done)
                        dve.tensor_scalar(low[:, t, lo:hi], low[:, t, lo:hi], rs_low[:, 2 * t + j:2 * t + j + 1], None,
                                          ALU.mult).then_inc(low_scaled, 1)

                def sum_squares(w):
                    dve.wait_ge(sq_ready, 4 * l + w + 1)
                    dim = B_DIM if w >= 2 else A_DIM
                    dve.reduce_sum(ss_h[:, w, :], sq[w % 2][:, 0:NT * HEADS * dim].rearrange("p (h c) -> p h c", c=dim),
                                   AX_X).then_inc(sq_used, 1)

                for w in range(2):
                    sum_squares(w)
                    for t in range(NT):
                        t_ = tile["qk"[w], l, t]
                        dve.wait_ge(drained[t_.bank], t_.done)
                    for piece in head_pieces(l, w):
                        piece()
                sum_squares(2)
                sum_squares(3)
                for t in range(NT):
                    for half in range(2):
                        t_ = tile["uq", l, t, half]
                        dve.wait_ge(drained[t_.bank], t_.done)

                def softmax_max(k):
                    t_ = tile["s", l, k]
                    full(t_)
                    if k >= 2:
                        dve.wait_ge(exp_done, 16 * l + k - 1)
                    scale = (A_DIM if k < HEADS else B_DIM) ** -0.5
                    ins = dve.scalar_tensor_tensor(out=sc[:, k % 2, :], in0=ps[t_.bank][:, 0:3 * P], scalar=scale,
                                                   in1=con("mask"), op0=ALU.mult, op1=ALU.add)
                    ins.then_inc(drained[t_.bank], 1)
                    dve.wait_ge(drained[t_.bank], t_.done)
                    dve.reduce_max(row_max[:, k % 2, 0:1], sc[:, k % 2, 0:P], AX_X)
                    step(dve.reduce_max(row_max[:, k % 2, 1:2], sc[:, k % 2, P:3 * P], AX_X))
                    dve.tensor_scalar(neg_max[:, k % 2, :], row_max[:, k % 2, :], -1.0, None, ALU.mult).then_inc(max_ready, 1)

                def take_y(quad):
                    b, q = quad // 2, quad % 2
                    dve.wait_ge(exp_done, 16 * l + 4 * quad + 4)
                    inv = row_inv[:, b, :, 4 * q:4 * q + 4]
                    step(dve.reciprocal(inv, row_sum[:, b, :, 4 * q:4 * q + 4]))
                    t_ = tile["y", l, quad]
                    full(t_)
                    dve.tensor_tensor(y[:, b, :, q * T:(q + 1) * T].rearrange("p t (h c) -> p t h c", c=A_DIM),
                                      ps[t_.bank][:, :].rearrange("p (t h c) -> p t h c", t=NT, c=A_DIM),
                                      inv.unsqueeze(3).broadcast_to([P, NT, 4, A_DIM]), ALU.mult).then_inc(drained[t_.bank], 1)

                pieces = head_pieces(l, 2) + head_pieces(l, 3)
                for k in range(16):
                    softmax_max(k)
                    for piece in pieces[2 * k:2 * k + 2]:
                        piece()
                    if k >= 5 and (k - 5) % 4 == 0:
                        take_y((k - 5) // 4)
                take_y(3)
                for m in range(DT):
                    t_ = tile["br", l, m]
                    full(t_)
                    dve.wait_ge(gate_ready, 4 * l + m // 2 + 1)
                    pair = prod[:, m % 2, :].rearrange("p (b c) -> p b c", b=2)
                    gates = gate.rearrange("p (b m) c -> p m b c", b=2)[:, m, :, :]
                    ins = dve.tensor_tensor(pair, view(t_.bank, 2, T), gates, ALU.mult)
                    ins.then_inc(drained[t_.bank], 1)
                    dve.wait_ge(drained[t_.bank], t_.done)
                    dve.tensor_tensor(merged[:, m, :], pair[:, 0, :], pair[:, 1, :], ALU.add).then_inc(merged_ready, 1)
                add_to_x("wo", l)
                norm(2 * l + 1, l, "ffn")

            def add_to_x(*key):
                for t in range(NT):
                    for half in range(2):
                        t_ = tile[(*key, t, half)]
                        full(t_)
                        xs = x[:, t, half * 512:(half + 1) * 512]
                        dve.tensor_tensor(xs, xs, ps[t_.bank][:, :], ALU.add).then_inc(drained[t_.bank], 1)

            def hidden(t_, n_silu, ft, n):
                dve.wait_ge(silu_done, n_silu)
                dve.tensor_tensor(hff[:, ft % 2, 0:n], sg[:, ft % 2, 0:n], ps[t_.bank][:, n:2 * n], ALU.mult).then_inc(
                    drained[t_.bank], 1)

            dve.wait_ge(x_in, 16)
            dve.wait_ge(const_in, 16)
            dve.wait_ge(route_in, 16 * 9)
            dve.wait_ge(gcol_set, 1)
            dve.tensor_copy(gcol[:, :], ps[7][:, 0:2 * GL]).then_inc(gcol_set, 1)
            dve.wait_ge(gcol_set, 2)
            mixer(0)
            with dve.Fori(0, DENSE_TURNS) as i:
                for s in range(4):
                    hidden(dense_gu[s].at(i, 1, 1), i * 4 + s + 1, s, T)
            for s in range(2):
                hidden(dense_gu[4 + s], 4 * DENSE_TURNS + s + 1, s, T)
            add_to_x("dense")
            mixer(1)

            t_ = tile["route"]
            full(t_)
            dve.memset(yTe[:, :, :], 0.0)
            dve.memset(route[:, 0:2, 0:1], -1.0)
            dve.memset(route[:, 2:4, 0:1], 0.0)
            dve.memset(route[:, 0:2, ITEMS + 1:ITEMS + 2], -1.0)
            dve.memset(route[:, 2:4, ITEMS + 1:ITEMS + 2], 0.0).then_inc(moe_zeroed, 1)
            lg, less, tmp16, chosen, ex = r16[0], r16[1], r16[2], r16[3], r16[4]
            dve.tensor_copy(lg, view(t_.bank, NT, NEXP)).then_inc(drained[t_.bank], 1)
            dve.wait_ge(drained[t_.bank], t_.done)
            other = lg.unsqueeze(2).broadcast_to([P, NT, NEXP, NEXP])
            own = lg.unsqueeze(3).broadcast_to([P, NT, NEXP, NEXP])
            lower = con("lower8").rearrange("p (e j) -> p e j", e=NEXP).unsqueeze(1).broadcast_to([P, NT, NEXP, NEXP])
            dve.tensor_tensor(r128[0], other, own, ALU.is_gt)
            step(dve.tensor_tensor(r128[1], other, own, ALU.is_equal))
            step(dve.tensor_tensor(r128[1], r128[1], lower, ALU.mult))
            step(dve.tensor_tensor(r128[0], r128[0], r128[1], ALU.add))
            step(dve.reduce_sum(tmp16, r128[0], AX_X))
            dve.tensor_scalar(chosen, tmp16, TOPK - 0.5, None, ALU.is_lt).then_inc(sel_bits, 1)
            step(dve.reduce_max(r2[0], lg, AX_X))
            dve.tensor_tensor(less, lg, r2[0].unsqueeze(2).broadcast_to([P, NT, NEXP]), ALU.subtract).then_inc(route_ready, 1)
            dve.wait_ge(sel_bits, 1)
            dve.wait_ge(route_exp, 1)
            step(dve.tensor_tensor(ex, ex, chosen, ALU.mult))
            step(dve.reduce_sum(r2[1], ex, AX_X))
            step(dve.reciprocal(r2[2], r2[1]))
            step(dve.tensor_tensor(ex, ex, r2[2].unsqueeze(2).broadcast_to([P, NT, NEXP]), ALU.mult))
            t_ = tile["rank"]
            full(t_)
            pos = ps[t_.bank][:, 0:16].rearrange("p (t e) -> p t e", t=NT)
            dve.scalar_tensor_tensor(out=tmp16, in0=pos, scalar=1.0, in1=chosen, op0=ALU.add, op1=ALU.mult)
            step(dve.reduce_max(r2[3][:, 0:1], ps[t_.bank][:, 16:24], AX_X))
            step(dve.tensor_scalar(r2[4][:, 0:1], r2[3][:, 0:1], float(CAP), float(ITEMS - NEXP), ALU.is_gt, ALU.mult))
            step(dve.tensor_scalar(r2[5][:, 0:1], r2[4][:, 0:1], float(NEXP), None, ALU.add))
            dve.tensor_copy(n_items[0:1, 0:1], r2[5][0:1, 0:1]).then_inc(items_known, 1)
            for k in range(PASSES):
                lo = 1 + k * NEXP
                dve.tensor_scalar(route[:, 0:2, lo:lo + NEXP], tmp16, -1.0 - k * CAP, None, ALU.add)
                last = dve.tensor_copy(route[:, 2:4, lo:lo + NEXP], ex)
            step(last)
            dve.sem_inc(drained[t_.bank], 1)
            slot_no = con("slot_no")

            def one_hot(dst, staged_, column, n_staged, gates, signal):
                dve.tensor_copy(staged_, route[:, :, bass.ds(column, 1)].rearrange("p q i -> p (q i)")).then_inc(staged, 1)
                dve.wait_ge(staged, n_staged)
                for t in range(NT):
                    last = dve.tensor_scalar(dst[:, t, :], slot_no, staged_[:, t:t + 1],
                                             staged_[:, 2 + t:3 + t] if gates else None, ALU.is_equal,
                                             *([ALU.mult] if gates else []))
                last.then_inc(signal, 1)

            def gathered(t_, g):
                full(t_)
                for j in range(4):
                    m = 4 * g + j
                    dve.tensor_scalar(hsel[:, m, :], ps[t_.bank][:, j * CAP:(j + 1) * CAP], gain(1, "ffn", m), None,
                                      ALU.mult).then_inc(drained[t_.bank], 1)

            one_hot(sel, stage, 1, 1, False, sel_ready)
            gathered(tile["gather0"][0], 0)

            def results(i):
                one_hot(selg, stage_g, i, i * 2 + 2, True, selg_ready)
                t_ = item_tile(i, "y", 0)
                full(t_)
                dve.tensor_copy(ye[:, 0:512], ps[t_.bank][0:CAP, :]).then_inc(drained[t_.bank], 1)

            def add_scatter(i):
                for j in range(4):
                    t_ = item_tile(i, "scatter", j)
                    full(t_)
                    t, half = j // 2, j % 2
                    xs = x[:, t, half * 512:(half + 1) * 512]
                    dve.tensor_tensor(xs, xs, ps[t_.bank][:, :], ALU.add).then_inc(drained[t_.bank], 1)

            def expert(i):
                silus = i * NFT + (NFT + 1)

                def mult(ft):
                    hidden(item_tile(i, "gu", ft), silus + ft, ft, CAP)

                mult(0)
                results(i)
                mult(1)
                add_scatter(i)
                for ft in range(2, NFT):
                    mult(ft)
                    if ft == NFT // 2:
                        one_hot(sel, stage, i + 2, i * 2 + 3, False, sel_ready)
                gathered(item_tile(i, "gather", 0), 0)
                t_ = item_tile(i, "yT", 0)
                full(t_)
                dve.tensor_copy(yTe[:, 0:4, :], view(t_.bank, 4, CAP)).then_inc(drained[t_.bank], 1)

            with dve.Fori(0, NEXP) as i:
                expert(i)
            n = dve.value_load(n_items[0:1, 0:1], min_val=NEXP, max_val=ITEMS)
            with dve.If(n > NEXP):
                with dve.Fori(NEXP, ITEMS) as i:
                    expert(i)
            results(n)
            add_scatter(n)

        @block.gpsimd
        def _(pool):
            pool.memset(half_neg[:, :], -0.5).then_inc(half_set, 1)
            pool.wait_ge(half_set, 1)

            def rstd(dst, src, parts, ms_sem, n, done):
                for lo, hi, width in parts:
                    last = pool.tensor_scalar(dst[:, lo:hi], src[:, lo:hi], 1.0 / width, EPS, ALU.mult, ALU.add)
                last.then_inc(ms_sem, 1)
                pool.wait_ge(ms_sem, n)
                w = parts[-1][1]
                pool.tensor_tensor(dst[:, 0:w], dst[:, 0:w], half_neg[:, 0:w], ALU.pow).then_inc(done, 1)

            def norm(n):
                pool.wait_ge(norm_sq, 2 * n + 2)
                rstd(rs_x, ss_x, [(0, 2, D)], norm_ms, n + 1, norm_rstd)

            for l in range(DEPTH):
                norm(2 * l)
                pool.wait_ge(low_sq, 4 * (l + 1))
                rstd(rs_low, ss_low, [(0, 1, Q_RANK), (1, 2, KV_RANK), (2, 3, Q_RANK), (3, 4, KV_RANK)], low_ms, l + 1,
                     low_rstd)
                for w in range(4):
                    if w == 2:
                        for t in range(NT):
                            t_ = tile["ckv", l, t]
                            pool.wait_ge(drained[t_.bank], t_.done)
                        for t in range(NT):
                            dst = qk_b[:, 1, t, :].rearrange("p (h c) -> p h c", c=B_DIM)[:, :, B_NOPE:]
                            src = low[:, t, Q_RANK + KV_RANK:LOW].unsqueeze(1).broadcast_to([P, HEADS, B_ROT])
                            last = pool.tensor_copy(dst, src)
                        last.then_inc(kr_placed, 1)
                    pool.wait_ge(sq_used, 4 * l + w + 1)
                    rstd(rs_h[:, w, :], ss_h[:, w, :], [(0, 16, B_DIM if w >= 2 else A_DIM)], head_ms, 4 * l + w + 1,
                         head_rstd)
                norm(2 * l + 1)


_INS = ["x", "attn_norm", "w_in", "moba_q_norm", "moba_k_norm", "mla_cq_norm", "w_uq", "mla_ckv_norm", "w_ukv",
        "mla_q_norm", "mla_k_norm", "w_branch_a", "w_branch_b", "w_out", "ffn_norm", "dense_w_gate_up",
        "dense_w_down", "router_w", "expert_w_gate_up", "expert_w_down"]


def build(nc, shapes):
    args = {n: nc.dram_tensor(f"in_{n}_dram", s, F32, kind="ExternalInput").ap() for n, s in shapes.items()}
    out = nc.dram_tensor("out_dram", (1, T, D), F32, kind="ExternalOutput").ap()
    trunk(nc, args, out)


def kernel(**inputs):
    import concourse.bacc as _bacc
    from concourse.bass_utils import run_bass_kernel_spmd as _run

    nc = _bacc.Bacc("TRN2", target_bir_lowering=False, num_devices=1)
    arrays = {n: np.ascontiguousarray(inputs[n]) for n in _INS}
    arrays["consts"] = constants()
    build(nc, {n: a.shape for n, a in arrays.items()})
    r = _run(nc, [{f"in_{n}_dram": a for n, a in arrays.items()}], core_ids=[0])
    return r.results[0]["out_dram"]
```

```python
import math
from contextlib import ExitStack

import numpy as np
import concourse.bass as bass
from concourse import mybir

F32 = mybir.dt.float32
F32R = mybir.dt.float32r
I32 = mybir.dt.int32
ALU = mybir.AluOpType
ACT = mybir.ActivationFunctionType
AX_X = mybir.AxisListType.X

P = 128
D = 1024
T = 256
NT = T // P
DT = D // P
DEPTH = 2
EPS = 1e-6
NEG = -1e30
THETA = 500000.0

HEADS = 8
A_DIM, A_ROT = 64, 16
B_NOPE, B_ROT, B_V = 64, 32, 64
B_DIM = B_NOPE + B_ROT
WIDTH = HEADS * A_DIM
Q_RANK, KV_RANK = 384, 256
LOW = Q_RANK + KV_RANK + B_ROT
OFF_Q, OFF_K, OFF_V, OFF_LOW = 0, WIDTH, 2 * WIDTH, 3 * WIDTH
OFF_GATE = OFF_LOW + LOW
DFF = 2816
GROUP = 256
NGROUP = DFF // GROUP
NFT = DFF // P
NEXP, TOPK = 8, 2
CAP = 128
PASSES = -(-T // CAP)
ITEMS = NEXP * PASSES

SLOTS = 4
SLOT = 3 * GROUP * DT

CONST = {}
_at = 0
for _name, _n in (("ident", P), ("mask", 3 * P), ("earlier", P), ("ones", P), ("slot_no", CAP),
                  ("cos_a", NT * A_ROT), ("sin_a", NT * A_ROT), ("cos_b", NT * B_ROT),
                  ("sin_b", NT * B_ROT), ("lower8", NEXP * NEXP)):
    CONST[_name] = (_at, _at + _n)
    _at += _n
NCONST = _at


def constants():
    c = np.zeros((P, NCONST), np.float32)

    def put(name, a):
        c[:, CONST[name][0]:CONST[name][1]] = a

    i = np.arange(P)
    put("ident", np.eye(P))
    diag = np.where(i[None, :] <= i[:, None], 0.0, NEG)
    put("mask", np.concatenate([diag, np.zeros((P, P)), diag], 1))
    put("earlier", i[:, None] < i[None, :])
    put("ones", 1.0)
    put("slot_no", np.arange(CAP)[None, :])
    for name, rot in (("a", A_ROT), ("b", B_ROT)):
        inv = (THETA ** (-np.arange(0, rot, 2, dtype=np.float64) / rot)).astype(np.float32)
        ang = (np.arange(T, dtype=np.float32)[:, None] * inv[None, :]).astype(np.float64)
        cos, sin = np.cos(ang), np.sin(ang)
        both = lambda a, b: np.concatenate([a, b], 1).reshape(NT, P, rot).transpose(1, 0, 2).reshape(P, NT * rot)
        put(f"cos_{name}", both(cos, cos))
        put(f"sin_{name}", both(-sin, sin))
    e = np.arange(NEXP)
    put("lower8", (e[None, :] < e[:, None]).reshape(1, -1))
    return c


class Tile:

    def __init__(self, bank, fill, free, done):
        self.bank, self.fill, self.free, self.done = bank, fill, free, done

    def at(self, i, fills, drains):
        return Tile(self.bank, i * fills + self.fill, i * drains + self.free, i * drains + self.done)


class Banks:

    def __init__(self, n):
        self.fills, self.drains, self.turn = [0] * n, [0] * n, 0

    def use(self, bank, evacs=1, fills=1):
        t = Tile(bank, self.fills[bank] + 1, self.drains[bank], self.drains[bank] + evacs)
        self.fills[bank] += fills
        self.drains[bank] += evacs
        return t

    def turns(self, n=8, evacs=1):
        self.turn = (self.turn + 1) % n
        return self.use(self.turn, evacs)


class Slots:

    def __init__(self, n):
        self.frees, self.loads = [0] * n, [0] * n
        self.last = [None] * n

    def use(self, slot, dmas, tile_key=None):
        before = self.last[slot]
        self.loads[slot] += 16 * dmas
        if tile_key is None:
            self.frees[slot] += 1
            self.last[slot] = self.frees[slot]
        else:
            self.last[slot] = tile_key
        return slot, before, self.loads[slot]


def trunk(nc, a, out):
    banks, slots = Banks(8), Slots(SLOTS)

    MIX = ["low", "q", "k", "v", "up", "g0", "g1", "g2", "g3", "bra", "brb", "wo0", "wo1"]
    MIX_DMAS = {"up": 2}
    MIX_LAST = {"low": ("ckv", 1), "q": ("q", 1), "k": ("k", 1), "v": ("v", 1), "up": ("ukv", 1, 1),
                "g0": ("gate", 1), "g1": ("gate", 3), "g2": ("gate", 5), "g3": ("gate", 7),
                "bra": ("br", DT - 1), "brb": ("br", DT - 1), "wo0": None, "wo1": ("wo", 1, 1)}
    chunk, tile = {}, {}

    def plan_norm(n):
        for dp in range(DT // 2):
            tile["hT", n, dp] = banks.turns(8, 2)

    def plan_mixer(l):
        for j, name in enumerate(MIX):
            chunk[l, name] = slots.use(
                j % SLOTS, MIX_DMAS.get(name, 1), MIX_LAST[name] and (MIX_LAST[name][0], l, *MIX_LAST[name][1:]))
        plan_norm(2 * l)
        for t in range(NT):
            tile["cq", l, t] = banks.turns()
            tile["ckv", l, t] = banks.turns()
        for name in "qkv":
            for t in range(NT):
                tile[name, l, t] = banks.turns()
        for j, evacs in enumerate((2, 1, 2)):
            tile["lowT", l, j] = banks.turns(8, evacs)
        for t in range(NT):
            for half in range(2):
                tile["uq", l, t, half] = banks.turns()
        for t in range(NT):
            for half in range(2):
                tile["ukv", l, t, half] = banks.turns(8, 2)
        for hp in range(4):
            tile["aT", l, hp] = banks.turns()
        banks.turn = 3
        tile["s", l, 0] = banks.turns(4)
        for k in range(16):
            if k + 1 < 16:
                tile["s", l, k + 1] = banks.turns(4)
            tile["pT", l, k] = banks.turns(4)
            if k % 2 == 0:
                tile["gate", l, k // 2] = banks.use(4 + k // 2 % 2)
            if k in (6, 7):
                for h in range(4 * (k - 6), 4 * (k - 6) + 4):
                    tile["bT", l, h] = banks.turns(4)
            if k % 4 == 0:
                tile["y", l, k // 4] = banks.use(6 + k // 4 % 2)
            if k == 10:
                for j in range(2):
                    tile["yT", l, 0, j] = banks.turns(4)
        for j in range(2):
            tile["yT", l, 1, j] = banks.turns(4)
        for m in range(DT):
            tile["br", l, m] = banks.turns(6)
        for t in range(NT):
            for half in range(2):
                tile["wo", l, t, half] = banks.turns(8)
        plan_norm(2 * l + 1)

    plan_mixer(0)
    DENSE_SLOTS = (1, 2)
    dense_before = [slots.last[s] for s in DENSE_SLOTS]
    dense_loads = [slots.loads[s] for s in DENSE_SLOTS]
    for s in range(2):
        slots.loads[DENSE_SLOTS[s]] += 32 * len(range(s, NGROUP, 2))
        slots.last[DENSE_SLOTS[s]] = "dense"
    DENSE_GU = [banks.use(t, 1, 0) for t in range(NT)]
    DENSE_TURN = banks.use(2)
    for _ in range(NGROUP - 1):
        for t in range(NT):
            banks.use(t, 1, 0)
        banks.use(2)
    for t in range(NT):
        for half in range(2):
            tile["dense", t, half] = banks.use(4 + 2 * t + half, 1, 0)
    plan_mixer(1)
    tile["route"] = banks.use(0)
    tile["rank"] = banks.use(1, 1)
    EXP_SLOTS = [(1, 2, 3, 0)[j % 4] for j in range(NGROUP)]
    exp_before, exp_loads = list(slots.last), list(slots.loads)
    EXP_USES = [EXP_SLOTS.count(s) for s in range(SLOTS)]
    DENSE_DOWNS = [16 * len(range(DENSE_SLOTS.index(s), NGROUP, 2)) if s in DENSE_SLOTS else 0 for s in range(SLOTS)]
    exp_tile = {}
    tile["gather0"] = [banks.use(6), banks.use(7)]
    tile["selT0"] = banks.use(3)
    tile["y0"] = [banks.use(4, 1, 0), banks.use(5, 1, 0)]
    base_fills, base_drains = list(banks.fills), list(banks.drains)
    for j in range(NGROUP):
        exp_tile["gu", j] = banks.use(j % 2, 1, 0)
        exp_tile["turn", j] = banks.use(2)
    for n in range(4):
        exp_tile["scatter", n] = banks.use(6 + n % 2)
    exp_tile["gather", 0], exp_tile["gather", 1] = banks.use(6), banks.use(7)
    exp_tile["selT",] = banks.use(3)
    exp_tile["y", 0], exp_tile["y", 1] = banks.use(4, 1, 0), banks.use(5, 1, 0)
    EXP_FILLS = [x - y for x, y in zip(banks.fills, base_fills)]
    EXP_DRAINS = [x - y for x, y in zip(banks.drains, base_drains)]

    UNITS = 6 * NGROUP
    UNIT = 1024

    def gu_at(j):
        return 0 if isinstance(j, int) and j == 0 else j * 6 - 2

    def dn_at(j):
        return UNITS - 2 if isinstance(j, int) and j == NGROUP - 1 else j * 6 + 8

    def prev_y(i):
        return [Tile(t_.bank, i * EXP_FILLS[t_.bank] + t_.fill, i * EXP_DRAINS[t_.bank] + t_.free,
                     i * EXP_DRAINS[t_.bank] + t_.done) for t_ in tile["y0"]]

    def own_gather(i):
        return [t_.at(i, EXP_FILLS[t_.bank], EXP_DRAINS[t_.bank]) for t_ in tile["gather0"]]

    def prev_selT(i):
        t_ = tile["selT0"]
        return t_.at(i, EXP_FILLS[t_.bank], EXP_DRAINS[t_.bank])

    def item_tile(i, *key):
        t = exp_tile[key]
        return t.at(i, EXP_FILLS[t.bank], EXP_DRAINS[t.bank])

    with ExitStack() as ctx:
        def sb(name, shape, dt=F32):
            return ctx.enter_context(nc.sbuf_tensor(name, shape, dt))

        def sem(name):
            return ctx.enter_context(nc.semaphore(name))

        ps = [ctx.enter_context(nc.psum_tensor(f"ps{b}", [P, 512], F32)) for b in range(8)]
        ring = [sb(f"ring{s}", [P, SLOT]) for s in range(SLOTS)]
        x = sb("x_res", [P, NT, D])
        h = sb("h_scaled", [P, NT, D])
        MIX_COLS = 20224

        def placed(name, shape):
            addr = -(-nc.sbuf_base // 32) * 32
            return addr, sb(name, shape)

        hT_at, hT = placed("hT", [P, DT, T])
        cst = sb("cst", [P, NCONST])
        gcol_rows = sb("gcol_rows", [2 * (2 * DT + 5), P])
        gcol = sb("gcol", [P, 2 * (2 * DT + 5)])
        g_heads = sb("g_heads", [P, DEPTH, 2 * A_DIM + 2 * B_DIM])
        router = sb("router", [P, DT, NEXP])
        small = sb("small", [P, 212])
        half_neg = sb("half_neg", [P, 16])
        mix_at, mix = placed("mix", [P, MIX_COLS])

        def con(name):
            return cst[:, CONST[name][0]:CONST[name][1]]

        ident = con("ident")
        ss_x, rs_x = small[:, 0:2], small[:, 2:4]
        ss_low, rs_low = small[:, 4:8], small[:, 8:12]
        neg_max = small[:, 12:16].rearrange("p (b c) -> p b c", b=2)
        row_max = small[:, 16:20].rearrange("p (b c) -> p b c", b=2)
        ss_h = small[:, 20:84].rearrange("p (w c) -> p w c", w=4)
        rs_h = small[:, 84:148].rearrange("p (w c) -> p w c", w=4)
        row_sum = small[:, 148:180].rearrange("p (b t h) -> p b t h", b=2, t=2)
        row_inv = small[:, 180:212].rearrange("p (b t h) -> p b t h", b=2, t=2)

        top = [0]

        def part(n):
            top[0] += n
            return top[0] - n

        o_low = part(2 * NT * WIDTH + 2 * 3 * P)
        low = mix[:, o_low:o_low + NT * LOW].rearrange("p (t c) -> p t c", t=NT)
        lowT = mix[:, o_low + NT * LOW:o_low + NT * LOW + 5 * T].rearrange("p (r c) -> p r c", r=5)
        y = mix[:, o_low:o_low + 2 * NT * WIDTH].rearrange("p (b t c) -> p b t c", b=2, t=NT)
        o_gate = part(2 * DT * T)
        gate = mix[:, o_gate:o_gate + 2 * DT * T].rearrange("p (m c) -> p m c", m=2 * DT)
        sq = [mix[:, o_gate + w * NT * HEADS * B_DIM:o_gate + (w + 1) * NT * HEADS * B_DIM] for w in range(2)]
        o_qka = part(2 * NT * WIDTH)
        qk_a = mix[:, o_qka:o_qka + 2 * NT * WIDTH].rearrange("p (w t c) -> p w t c", w=2, t=NT)
        yT = mix[:, o_qka:o_qka + 8 * T].rearrange("p (m c) -> p m c", m=8)
        o_v = part(2 * NT * WIDTH)
        v = mix[:, o_v:o_v + 2 * NT * WIDTH].rearrange("p (b t c) -> p b t c", b=2, t=NT)
        o_qkb = part(2 * NT * HEADS * B_DIM)
        qk_b = mix[:, o_qkb:o_qkb + 2 * NT * HEADS * B_DIM].rearrange("p (w t c) -> p w t c", w=2, t=NT)
        o_ta = part(4 * 4 * P)
        qkT_a = mix[:, o_ta:o_ta + 4 * 4 * P].rearrange("p (g c) -> p g c", g=4)
        o_tb = part(HEADS * 4 * P)
        qkT_b = mix[:, o_tb:o_tb + HEADS * 4 * P].rearrange("p (g c) -> p g c", g=HEADS)
        merged = mix[:, o_tb:o_tb + DT * T].rearrange("p (m c) -> p m c", m=DT)
        prod = mix[:, o_tb + DT * T:o_tb + DT * T + 4 * T].rearrange("p (b c) -> p b c", b=2)
        hflat = h[:, :, :].rearrange("p t c -> p (t c)")
        sc = hflat[:, 0:768].rearrange("p (b c) -> p b c", b=2)
        pr = hflat[:, 768:1536].rearrange("p (b c) -> p b c", b=2)
        rot_tmp = hflat[:, 1536:2048]
        pT = mix[:, o_low + 2 * NT * WIDTH:o_low + 2 * NT * WIDTH + 2 * 3 * P].rearrange("p (b c) -> p b c", b=2)
        assert top[0] <= MIX_COLS, top[0]

        top[0] = 0
        o = part(NT * GROUP)
        sg = mix[:, o:o + NT * GROUP].rearrange("p (t c) -> p t c", t=NT)
        o = part(NT * GROUP)
        hff = mix[:, o:o + NT * GROUP].rearrange("p (t c) -> p t c", t=NT)
        o = part(NT * CAP)
        sel = mix[:, o:o + NT * CAP].rearrange("p (t c) -> p t c", t=NT)
        o = part(4 * (ITEMS + 2))
        route = mix[:, o:o + 4 * (ITEMS + 2)].rearrange("p (q i) -> p q i", q=4)
        o = part(8)
        stage, stage_g = mix[:, o:o + 4], mix[:, o + 4:o + 8]
        o = part(16 * 8)
        r16 = [mix[:, o + 16 * j:o + 16 * j + 16].rearrange("p (t e) -> p t e", t=NT) for j in range(8)]
        o = part(2 * 128)
        r128 = [mix[:, o + 128 * j:o + 128 * j + 128].rearrange("p (t e j) -> p t e j", t=NT, e=NEXP) for j in range(2)]
        o = part(16)
        r2 = [mix[:, o + 2 * j:o + 2 * j + 2] for j in range(8)]
        at = [mix_at + 4 * top[0]]

        def sr(name, shape):
            t_ = nc.alloc_sbuf_tensor_at(name, shape, F32R, offset=at[0])
            at[0] += 4 * math.prod(shape[1:])
            return t_

        hT_parts = [sr(f"hT_{p_}", [P, DT, T]) for p_ in ("hi", "lo")]
        w_hi, w_lo = ([sr(f"w_{p_}{q}", [P, UNIT]) for q in range(6)] for p_ in ("hi", "lo"))
        g_row_at = (at[0] - mix_at) // 4 - D
        g_row = mix[:, g_row_at:g_row_at + D]
        hffT = [sr(f"hffT_{p_}", [P, GROUP // P, T]) for p_ in ("hi", "lo")]
        selT = sr("selT", [CAP, T])
        zero = sr("zero", [P, P])
        n_items = nc.alloc_sbuf_tensor_at("n_items", [1, 1], I32, offset=at[0])
        at[0] += 4
        assert at[0] <= mix_at + 4 * MIX_COLS, (at[0], mix_at + 4 * MIX_COLS)
        ye = [nc.alloc_sbuf_tensor_at(f"ye_{p_}", [CAP, D], F32R, offset=hT_at + 4 * D * n)
              for n, p_ in enumerate(("hi", "lo"))]

        loaded = [sem(f"slot{s}_loaded") for s in range(SLOTS)]
        freed = [sem(f"slot{s}_freed") for s in range(SLOTS)]
        filled = [sem(f"bank{b}_filled") for b in range(8)]
        drained = [sem(f"bank{b}_drained") for b in range(8)]
        x_in = sem("x_in")
        const_in = sem("const_in")
        gain_in = sem("gain_in")
        half_set = sem("half_set")
        gcol_set = sem("gcol_set")
        norm_sq = sem("norm_sq")
        norm_ms = sem("norm_ms")
        norm_rstd = sem("norm_rstd")
        h_scaled = sem("h_scaled")
        low_sq = sem("low_sq")
        low_ms = sem("low_ms")
        low_rstd = sem("low_rstd")
        low_scaled = sem("low_scaled")
        kr_placed = sem("kr_placed")
        kb_copied = sem("kb_copied")
        sq_ready = sem("sq_ready")
        sq_used = sem("sq_used")
        head_ms = sem("head_ms")
        head_rstd = sem("head_rstd")
        qk_normed = sem("qk_normed")
        max_ready = sem("max_ready")
        exp_done = sem("exp_done")
        pv_done = sem("pv_done")
        gate_copied = sem("gate_copied")
        gate_ready = sem("gate_ready")
        merged_ready = sem("merged_ready")
        silu_done = sem("silu_done")
        loaded_down = [sem(f"slot{s}_down_loaded") for s in range(SLOTS)]
        hi_ready = sem("hi_ready")
        split_ready = sem("split_ready")
        unit_used = sem("unit_used")
        turned_hi = sem("turned_hi")
        gathered_hi = sem("gathered_hi")
        ye_hi = sem("ye_hi")
        scattered = sem("scattered")
        zero_set = sem("zero_set")
        g_row_in = sem("g_row_in")
        h_gained = sem("h_gained")
        route_in = sem("route_in")
        route_exp = sem("route_exp")
        sel_bits = sem("sel_bits")
        route_ready = sem("route_ready")
        items_known = sem("items_known")
        moe_zeroed = sem("moe_zeroed")
        sel_ready = sem("sel_ready")
        staged = sem("staged")
        dve_step = sem("dve_step")
        out_done = sem("out_done")

        def view(b, *shape):
            n = math.prod(shape)
            flat = ps[b][:, 0:n]
            return flat if len(shape) == 1 else flat.rearrange("p (a c) -> p a c", a=shape[0])

        def w_view(slot, kts, cols, at=0):
            return ring[slot][:, at:at + kts * cols].rearrange("p (k c) -> p k c", k=kts)

        GU = DT * GROUP

        G0 = {"attn": 0, "ffn": DT, "cq": 2 * DT, "ckv": 2 * DT + 3}
        GN = {"attn": DT, "ffn": DT, "cq": 3, "ckv": 2}
        GL = 2 * DT + 5

        def gain(l, name, j):
            c = DEPTH * G0[name] + l * GN[name] + j
            return gcol[:, c:c + 1]

        GAIN_ROW_DMAS = 4

        block = ctx.enter_context(nc.Block())

        @block.sync
        def _(sp):
            def rows(ap):
                return ap.rearrange("(k p) c -> p k c", p=P)

            def until_free(slot, before):
                if isinstance(before, int):
                    sp.wait_ge(freed[slot], before)
                elif before == "dense":
                    sp.wait_ge(split_ready, UNITS)
                elif before is not None:
                    sp.wait_ge(filled[tile[before].bank], tile[before].fill)

            def load_mixer(l, names):
                w_in = a["w_in"][l]
                for name in names:
                    slot, before, _ = chunk[l, name]
                    until_free(slot, before)
                    if name == "up":
                        n = 3 * HEADS * B_DIM
                        parts = [(w_view(slot, 3, HEADS * B_DIM), rows(a["w_uq"][l])),
                                 (w_view(slot, 2, D, n), rows(a["w_ukv"][l]))]
                    elif name[:2] == "br":
                        w = a["w_branch_a"] if name == "bra" else a["w_branch_b"]
                        parts = [(w_view(slot, 4, D), rows(w[l]))]
                    elif name[:2] == "wo":
                        j = int(name[2])
                        parts = [(w_view(slot, 4, D), rows(a["w_out"][l, j * WIDTH:(j + 1) * WIDTH, :]))]
                    else:
                        at, n = {"low": (OFF_LOW, LOW), "q": (OFF_Q, WIDTH), "k": (OFF_K, WIDTH),
                                 "v": (OFF_V, WIDTH)}.get(name) or (OFF_GATE + WIDTH * int(name[1]), WIDTH)
                        parts = [(w_view(slot, DT, n), rows(w_in[:, at:at + n]))]
                    for dst, src in parts:
                        sp.dma_start(dst, src).then_inc(loaded[slot], 16)

            def load_gate_up(slot, gate_up, j):
                dst = ring[slot][:, 0:2 * GU].rearrange("p (k s c) -> p k s c", k=DT, s=2)
                for n in range(2):
                    sp.dma_start(dst[:, :, n, :], rows(gate_up[:, bass.ds(j * GROUP + n * DFF, GROUP)])).then_inc(
                        loaded[slot], 16)

            def load_down(slot, down, j):
                sp.dma_start(w_view(slot, GROUP // P, D, 2 * GU), rows(down[bass.ds(j * GROUP, GROUP), :])).then_inc(
                    loaded_down[slot], 16)

            sp.dma_start(x[:, :, :], a["x"][0].rearrange("(t p) c -> p t c", p=P)).then_inc(x_in, 16)
            load_mixer(0, MIX[:1])
            sp.wait_ge(gain_in, 16 * GAIN_ROW_DMAS)
            sp.wait_ge(const_in, 16)
            sp.wait_ge(route_in, 16 * 5)
            load_mixer(0, MIX[1:])
            gu, dn = a["dense_w_gate_up"][0], a["dense_w_down"][0]
            even, odd = DENSE_SLOTS
            until_free(even, dense_before[0])
            load_gate_up(even, gu, 0)
            load_down(even, dn, 0)
            until_free(odd, dense_before[1])
            load_gate_up(odd, gu, 1)

            def split(n):
                sp.wait_ge(split_ready, n)

            split(gu_at(0) + 4)
            load_gate_up(even, gu, 2)
            load_down(odd, dn, 1)
            with sp.Fori(0, (NGROUP - 3) // 2) as i:
                for g, d, s_g, s_d in ((i * 2 + 3, i * 2 + 2, odd, even), (i * 2 + 4, i * 2 + 3, even, odd)):
                    split(gu_at(g - 2) + 4)
                    load_gate_up(s_g, gu, g)
                    split(dn_at(d - 2) + 2)
                    load_down(s_d, dn, d)
            split(dn_at(NGROUP - 3) + 2)
            load_down(even, dn, NGROUP - 1)
            load_mixer(1, MIX)

            def load_experts(k):
                with sp.Fori(0 if k else 1, NEXP) as e:
                    load_expert(e, e + k * NEXP)

            def load_expert(e, item):
                gu, dn = a["expert_w_gate_up"][0, e], a["expert_w_down"][0, e]
                for j, slot in enumerate(EXP_SLOTS):
                    earlier = [g for g in range(j) if EXP_SLOTS[g] == slot]
                    if earlier:
                        base, g = (item + 1) * UNITS, earlier[-1]
                    else:
                        base, g = item * UNITS, NGROUP - 1 - EXP_SLOTS[::-1].index(slot)
                    fresh = isinstance(item, int) and not earlier
                    if fresh:
                        until_free(slot, exp_before[slot])
                    else:
                        sp.wait_ge(split_ready, base + (gu_at(g) + 4))
                    load_gate_up(slot, gu, j)
                    if not fresh:
                        sp.wait_ge(split_ready, base + (dn_at(g) + 2))
                    load_down(slot, dn, j)

            load_expert(0, 0)
            load_experts(0)
            sp.wait_ge(items_known, 1)
            n = sp.value_load(n_items[0:1, 0:1], min_val=NEXP, max_val=ITEMS)
            with sp.If(n > NEXP):
                for k in range(1, PASSES):
                    load_experts(k)
            last = item_tile(n, "scatter", 3)
            sp.wait_ge(drained[last.bank], last.done)
            sp.dma_start(out[0].rearrange("(t p) c -> p t c", p=P), x[:, :, :]).then_inc(out_done, 16)
            sp.wait_ge(out_done, 16)

        @block.tensor
        def _(pe):
            def fill(t):
                pe.wait_ge(drained[t.bank], t.free)

            def start(t):
                if t.free:
                    fill(t)

            def evacuated(t):
                pe.wait_ge(drained[t.bank], t.done)

            def arrived(c):
                pe.wait_ge(loaded[c[0]], c[2])

            def norm_transposes(n):
                pe.wait_ge(h_scaled, 2 * n + 2)
                for dp in range(DT // 2):
                    t_ = tile["hT", n, dp]
                    start(t_)
                    for j in range(2):
                        for t in range(NT):
                            last = pe.transpose(ps[t_.bank][:, (2 * j + t) * P:(2 * j + t + 1) * P],
                                                h[:, t, (2 * dp + j) * P:(2 * dp + j + 1) * P], ident)
                    last.then_inc(filled[t_.bank], 1)

            def hT_ready(n):
                for dp in range(DT // 2):
                    evacuated(tile["hT", n, dp])

            def by_tokens(t_, t, w, cols, src, k0=0, kn=DT, first=True, final=True):
                for k in range(kn):
                    last = pe.matmul(ps[t_.bank][:, cols[0]:cols[1]], src[:, k0 + k, t * P:(t + 1) * P], w[k],
                                     start=first and k == 0, stop=final and k == kn - 1)
                return last

            def mixer(l):
                norm_transposes(2 * l)
                hT_ready(2 * l)
                c = chunk[l, "low"]
                arrived(c)
                w = w_view(c[0], DT, LOW)
                for t in range(NT):
                    for name, lo, hi in (("cq", 0, Q_RANK), ("ckv", Q_RANK, LOW)):
                        t_ = tile[name, l, t]
                        start(t_)
                        last = by_tokens(t_, t, [w[:, k, lo:hi] for k in range(DT)], (0, hi - lo), hT)
                        last.then_inc(filled[t_.bank], 1)
                for name in "qkv":
                    c = chunk[l, name]
                    arrived(c)
                    w = w_view(c[0], DT, WIDTH)
                    for t in range(NT):
                        t_ = tile[name, l, t]
                        start(t_)
                        last = by_tokens(t_, t, [w[:, k, :] for k in range(DT)], (0, WIDTH), hT)
                        last.then_inc(filled[t_.bank], 1)
                pe.wait_ge(low_scaled, 4 * (l + 1))
                for j, rs in enumerate(((0, 1), (2,), (3, 4))):
                    t_ = tile["lowT", l, j]
                    start(t_)
                    for n, r in enumerate(rs):
                        for t in range(NT):
                            last = pe.transpose(ps[t_.bank][:, (2 * n + t) * P:(2 * n + t + 1) * P],
                                                low[:, t, r * P:(r + 1) * P], ident)
                    last.then_inc(filled[t_.bank], 1)
                for j in range(3):
                    evacuated(tile["lowT", l, j])
                c = chunk[l, "up"]
                arrived(c)
                wq = w_view(c[0], 3, HEADS * B_DIM)
                wkv = w_view(c[0], 2, D, 3 * HEADS * B_DIM)
                for name, w, k0, kn, n in (("uq", wq, 0, 3, HEADS * B_DIM // 2), ("ukv", wkv, 3, 2, D // 2)):
                    for t in range(NT):
                        for half in range(2):
                            t_ = tile[name, l, t, half]
                            start(t_)
                            last = by_tokens(t_, t, [w[:, k, half * n:(half + 1) * n] for k in range(kn)], (0, n),
                                             lowT, k0, kn)
                            last.then_inc(filled[t_.bank], 1)
                pe.wait_ge(qk_normed, 4 * l + 2)
                for hp in range(4):
                    t_ = tile["aT", l, hp]
                    start(t_)
                    for w in range(2):
                        for t in range(NT):
                            last = pe.transpose(ps[t_.bank][:, (2 * w + t) * P:(2 * w + t + 1) * P],
                                                qk_a[:, w, t, hp * P:(hp + 1) * P], ident)
                    last.then_inc(filled[t_.bank], 1)

                def q_k(k):
                    if k < HEADS:
                        lo = (k % 2) * A_DIM
                        both = qkT_a[lo:lo + A_DIM, k // 2, :]
                    else:
                        both = qkT_b[0:B_DIM, k - HEADS, :]
                    return both[:, 0:T], both[:, T:2 * T]

                def scores(k):
                    evacuated(tile["aT", l, k // 2] if k < HEADS else tile["bT", l, k - HEADS])
                    t_ = tile["s", l, k]
                    start(t_)
                    q, key = q_k(k)
                    pe.matmul(ps[t_.bank][:, 0:P], q[:, 0:P], key[:, 0:P], start=True, stop=True)
                    pe.matmul(ps[t_.bank][:, P:3 * P], q[:, P:T], key, start=True, stop=True).then_inc(filled[t_.bank], 1)

                def turn_probs(k):
                    pe.wait_ge(exp_done, 16 * l + k + 1)
                    t_ = tile["pT", l, k]
                    start(t_)
                    for j in range(3):
                        last = pe.transpose(ps[t_.bank][:, j * P:(j + 1) * P], pr[:, k % 2, j * P:(j + 1) * P], ident)
                    last.then_inc(filled[t_.bank], 1)

                def gates(k):
                    t_ = tile["gate", l, k // 2]
                    c = chunk[l, f"g{k // 4}"]
                    if k % 2 == 0:
                        start(t_)
                    if k % 4 == 0:
                        arrived(c)
                    w = w_view(c[0], DT, WIDTH)
                    for kt in range(DT):
                        last = pe.matmul(ps[t_.bank][:, (k % 2) * T:(k % 2 + 1) * T], w[:, kt, (k % 4) * P:(k % 4 + 1) * P],
                                         hT[:, kt, :], start=kt == 0, stop=kt == DT - 1)
                    if k % 2:
                        last.then_inc(filled[t_.bank], 1)

                def turn_b(hd):
                    pe.wait_ge(qk_normed, 4 * l + 4)
                    t_ = tile["bT", l, hd]
                    start(t_)
                    for w in range(2):
                        for t in range(NT):
                            last = pe.transpose(ps[t_.bank][0:B_DIM, (2 * w + t) * P:(2 * w + t + 1) * P],
                                                qk_b[:, w, t, hd * B_DIM:(hd + 1) * B_DIM], ident)
                    last.then_inc(filled[t_.bank], 1)

                def values(k):
                    t_ = tile["y", l, k // 4]
                    evacuated(tile["pT", l, k])
                    if k % 4 == 0:
                        start(t_)
                    if k == 0:
                        for t in range(NT):
                            evacuated(tile["v", l, t])
                    if k == HEADS:
                        for t in range(NT):
                            for half in range(2):
                                evacuated(tile["ukv", l, t, half])
                    vv = v[:, k // HEADS, :, (k % HEADS) * A_DIM:(k % HEADS + 1) * A_DIM]
                    o0 = (k % 4) * A_DIM
                    o1 = T + o0
                    bank = ps[t_.bank]
                    pe.matmul(bank[:, o0:o0 + A_DIM], pT[:, k % 2, 0:P], vv[:, 0, :], start=True, stop=True)
                    pe.matmul(bank[:, o1:o1 + A_DIM], pT[:, k % 2, P:2 * P], vv[:, 0, :], start=True, stop=False)
                    last = pe.matmul(bank[:, o1:o1 + A_DIM], pT[:, k % 2, 2 * P:3 * P], vv[:, 1, :], start=False, stop=True)
                    if k % 4 == 3:
                        last.then_inc(filled[t_.bank], 1)
                    else:
                        last.then_inc(pv_done, 1)

                def turn_y(b):
                    for quad in range(2):
                        evacuated(tile["y", l, 2 * b + quad])
                    for j in range(2):
                        t_ = tile["yT", l, b, j]
                        start(t_)
                        for m in range(2):
                            for t in range(NT):
                                last = pe.transpose(ps[t_.bank][:, (2 * m + t) * P:(2 * m + t + 1) * P],
                                                    y[:, b, t, (2 * j + m) * P:(2 * j + m + 1) * P], ident)
                        last.then_inc(filled[t_.bank], 1)

                scores(0)
                for k in range(16):
                    if k + 1 < 16:
                        scores(k + 1)
                    turn_probs(k)
                    gates(k)
                    if k in (6, 7):
                        for hd in range(4 * (k - 6), 4 * (k - 6) + 4):
                            turn_b(hd)
                    values(k)
                    if k == 10:
                        turn_y(0)
                turn_y(1)
                wb = []
                for name in ("bra", "brb"):
                    c = chunk[l, name]
                    arrived(c)
                    wb.append(w_view(c[0], 4, D))
                for b in range(2):
                    for j in range(2):
                        evacuated(tile["yT", l, b, j])
                for m in range(DT):
                    t_ = tile["br", l, m]
                    start(t_)
                    for b in range(2):
                        for kt in range(4):
                            last = pe.matmul(ps[t_.bank][:, b * T:(b + 1) * T], wb[b][:, kt, m * P:(m + 1) * P],
                                             yT[:, 4 * b + kt, :], start=kt == 0, stop=kt == 3)
                    last.then_inc(filled[t_.bank], 1)
                for j in range(2):
                    c = chunk[l, f"wo{j}"]
                    arrived(c)
                    w = w_view(c[0], 4, D)
                    for kk in range(4):
                        kt = 4 * j + kk
                        pe.wait_ge(merged_ready, DT * l + kt + 1)
                        for t in range(NT):
                            for half in range(2):
                                t_ = tile["wo", l, t, half]
                                if kt == 0:
                                    start(t_)
                                last = pe.matmul(ps[t_.bank][:, :], merged[:, kt, t * P:(t + 1) * P],
                                                 w[:, kk, half * 512:(half + 1) * 512], start=kt == 0, stop=kt == DT - 1)
                                if kt == DT - 1:
                                    last.then_inc(filled[t_.bank], 1)
                    if j == 0:
                        last.then_inc(freed[c[0]], 1)
                norm_transposes(2 * l + 1)
                hT_ready(2 * l + 1)

            def split_unit(n, at):
                pe.wait_ge(split_ready, n + (at + 1))

            def three(out_, left, w, cols, first, final):
                (l_hi, l_lo), (w_hi_, w_lo_) = left, w
                pe.matmul(out_, l_hi, w_hi_[:, cols], start=first, stop=False, skip_group_check=True)
                pe.matmul(out_, l_hi, w_lo_[:, cols], start=False, stop=False, skip_group_check=True)
                return pe.matmul(out_, l_lo, w_hi_[:, cols], start=False, stop=final, skip_group_check=True)

            def gate_up(n, at, tiles):
                for q in range(4):
                    split_unit(n, at + q)
                    for t, t_ in enumerate(tiles):
                        if q == 0:
                            fill(t_)
                        for kk in range(2):
                            left = [part_[:, 2 * q + kk, t * P:(t + 1) * P] for part_ in hT_parts]
                            last = three(ps[t_.bank][:, :], left, (w_hi[q], w_lo[q]), slice(kk * 512, (kk + 1) * 512),
                                         q + kk == 0, q == 3 and kk == 1)
                    last.then_inc(unit_used, 1)

            def down(n, at, turned, outs, first, final):
                evacuated(turned)
                for s in range(2):
                    split_unit(n, at + s)
                    for m, o in enumerate(outs):
                        t, half = m // 2, m % 2
                        if first and s == 0:
                            fill(o)
                        left = [part_[:, s, t * P:(t + 1) * P] for part_ in hffT]
                        last = three(ps[o.bank][:, :], left, (w_hi[4 + s], w_lo[4 + s]), slice(half * 512, (half + 1) * 512),
                                     first and s == 0, final and s == 1)
                    last.then_inc(unit_used, 1)

            def turn_hidden(ready, turned, tiles):
                for t_ in ready:
                    evacuated(t_)
                fill(turned)
                for s in range(2):
                    for t in range(tiles):
                        last = pe.transpose(ps[turned.bank][:, s * T + t * P:s * T + (t + 1) * P],
                                            hff[:, t, s * P:(s + 1) * P], ident)
                last.then_inc(filled[turned.bank], 1)

            def dense():
                gu_tiles = lambda j: [t_.at(j, 1, 1) for t_ in DENSE_GU]
                turned = lambda j: DENSE_TURN.at(j, 1, 1)
                outs = [tile["dense", t, half] for t in range(NT) for half in range(2)]

                def step(j):
                    gate_up(0, gu_at(j), gu_tiles(j))
                    down(0, dn_at(j - 1), turned(j - 1), outs, False, False)
                    turn_hidden(gu_tiles(j), turned(j), NT)

                gate_up(0, 0, gu_tiles(0))
                pe.wait_ge(zero_set, 1)
                for o in outs:
                    fill(o)
                    pe.matmul(ps[o.bank][:, :], zero[:, :], zero[:, :].unsqueeze(1).broadcast_to([P, 4, P]),
                              start=True, stop=False, skip_group_check=True)
                turn_hidden(gu_tiles(0), turned(0), NT)
                with pe.Fori(0, NGROUP // 2) as i:
                    step(i * 2 + 1)
                    step(i * 2 + 2)
                down(0, dn_at(NGROUP - 1), turned(NGROUP - 1), outs, False, True)

            def routing():
                t_ = tile["route"]
                start(t_)
                for t in range(NT):
                    for kt in range(DT):
                        last = pe.matmul(ps[t_.bank][:, t * NEXP:(t + 1) * NEXP], hT[:, kt, t * P:(t + 1) * P],
                                         router[:, kt, :], start=kt == 0, stop=kt == DT - 1)
                last.then_inc(filled[t_.bank], 1)
                pe.wait_ge(sel_bits, 1)
                t_ = tile["rank"]
                start(t_)
                chosen = r16[3]
                before, every = con("earlier"), con("ones")
                bank = ps[t_.bank]
                pe.matmul(bank[:, 0:8], before, chosen[:, 0, :], start=True, stop=True)
                pe.matmul(bank[:, 8:16], every, chosen[:, 0, :], start=True, stop=False)
                pe.matmul(bank[:, 8:16], before, chosen[:, 1, :], start=False, stop=True)
                pe.matmul(bank[:, 16:24], every, chosen[:, 0, :], start=True, stop=False)
                pe.matmul(bank[:, 16:24], every, chosen[:, 1, :], start=False, stop=True).then_inc(filled[t_.bank], 1)

            def gather(n_sel, tiles, sel_tile):
                pe.wait_ge(sel_ready, n_sel)
                for g, t_ in enumerate(tiles):
                    fill(t_)
                    for j in range(4):
                        for t in range(NT):
                            last = pe.matmul(ps[t_.bank][:, j * CAP:(j + 1) * CAP],
                                             h[:, t, (4 * g + j) * P:(4 * g + j + 1) * P], sel[:, t, :],
                                             start=t == 0, stop=t == NT - 1)
                    last.then_inc(filled[t_.bank], 1)

                fill(sel_tile)
                for t in range(NT):
                    last = pe.transpose(ps[sel_tile.bank][:, t * P:(t + 1) * P], sel[:, t, :], ident)
                last.then_inc(filled[sel_tile.bank], 1)

            def scatter(i):
                pe.wait_ge(ye_hi, i * 2 + 2)
                for t_ in prev_y(i):
                    evacuated(t_)
                evacuated(prev_selT(i - 1))
                for t in range(NT):
                    for half in range(2):
                        t_ = item_tile(i, "scatter", 2 * t + half)
                        fill(t_)
                        for n, part_ in enumerate(ye):
                            last = pe.matmul(ps[t_.bank][:, :], selT[:, t * P:(t + 1) * P],
                                             part_[:, half * 512:(half + 1) * 512], start=n == 0, stop=n == 1)
                        last.then_inc(filled[t_.bank], 1)

            def expert(i):
                n = (i + 1) * UNITS
                outs = [item_tile(i, "y", half) for half in range(2)]
                hidden = lambda j: [item_tile(i, "gu", j)]
                turned = lambda j: item_tile(i, "turn", j)
                for t_ in own_gather(i):
                    evacuated(t_)
                gate_up(n, 0, hidden(0))
                turn_hidden(hidden(0), turned(0), 1)
                for j in range(1, NGROUP):
                    gate_up(n, gu_at(j), hidden(j))
                    if j == 1:
                        scatter(i)
                    down(n, dn_at(j - 1), turned(j - 1), outs, j == 1, False)
                    turn_hidden(hidden(j), turned(j), 1)
                gather(i + 2, [item_tile(i, "gather", g) for g in range(2)], item_tile(i, "selT"))
                down(n, dn_at(NGROUP - 1), turned(NGROUP - 1), outs, False, True)

            pe.wait_ge(const_in, 16)
            pe.wait_ge(gain_in, 16 * GAIN_ROW_DMAS)
            pe.transpose(ps[7][:, 0:2 * GL], gcol_rows[:, :], ident[0:2 * GL, 0:2 * GL]).then_inc(gcol_set, 1)
            mixer(0)
            dense()
            mixer(1)
            routing()
            pe.wait_ge(moe_zeroed, 1)
            for t_ in tile["y0"]:
                fill(t_)
                pe.matmul(ps[t_.bank][:, :], zero[:, :], zero[:, :].unsqueeze(1).broadcast_to([P, 4, P]),
                          start=True, stop=True)
            pe.wait_ge(h_gained, NT)
            gather(1, tile["gather0"], tile["selT0"])
            with pe.Fori(0, NEXP) as i:
                expert(i)
            pe.wait_ge(items_known, 1)
            n = pe.value_load(n_items[0:1, 0:1], min_val=NEXP, max_val=ITEMS)
            with pe.If(n > NEXP):
                with pe.Fori(NEXP, ITEMS) as i:
                    expert(i)
            scatter(n)

        @block.scalar
        def _(act):
            def full(t_):
                act.wait_ge(filled[t_.bank], t_.fill)

            act.dma_start(cst[:, :], a["consts"]).then_inc(const_in, 16)
            for name, w, n in (("attn", "attn_norm", DT), ("ffn", "ffn_norm", DT), ("cq", "mla_cq_norm", 3),
                               ("ckv", "mla_ckv_norm", 2)):
                r = DEPTH * G0[name]
                act.dma_start(gcol_rows[r:r + DEPTH * n, :], a[w].rearrange("l (r c) -> (l r) c", c=P)).then_inc(gain_in, 16)
            at = 0
            for w, n in (("moba_q_norm", A_DIM), ("moba_k_norm", A_DIM), ("mla_q_norm", B_DIM), ("mla_k_norm", B_DIM)):
                act.dma_start(g_heads[:, :, at:at + n], a[w].partition_broadcast(P)).then_inc(route_in, 16)
                at += n
            act.dma_start(router[:, :, :], a["router_w"][0].rearrange("(k p) e -> p k e", p=P)).then_inc(route_in, 16)

            def copy_out(dst, t_, src):
                act.copy(dst, src).then_inc(drained[t_.bank], 1)

            def norm(n, l, gain_name, parts=False):
                for t in range(NT):
                    act.activation(h[:, t, :], x[:, t, :], ACT.Square, accum_out=ss_x[:, t:t + 1]).then_inc(norm_sq, 1)
                for dp in range(DT // 2) if parts else range(1, DT // 2, 2):
                    t_ = tile["hT", n, dp]
                    full(t_)
                    if parts:
                        for j in range(2):
                            act.mul(hT_parts[0][:, 2 * dp + j, :], view(t_.bank, 2, T)[:, j, :],
                                    gain(l, gain_name, 2 * dp + j)).then_inc(gathered_hi, 1)
                        continue
                    for j in range(2):
                        act.mul(hT[:, 2 * dp + j, :], view(t_.bank, 2, T)[:, j, :],
                                gain(l, gain_name, 2 * dp + j)).then_inc(drained[t_.bank], 1)

            def mixer(l):
                norm(2 * l, l, "attn")
                for t in range(NT):
                    for name, j, n, at in (("cq", 0, Q_RANK, 0), ("ckv", 1, KV_RANK, Q_RANK)):
                        t_ = tile[name, l, t]
                        full(t_)
                        c = 2 * t + j
                        act.activation(mix[:, o_gate + c * Q_RANK:o_gate + c * Q_RANK + n], ps[t_.bank][:, 0:n], ACT.Square,
                                       accum_out=ss_low[:, c:c + 1]).then_inc(low_sq, 1)
                        m = n if name == "cq" else LOW - Q_RANK
                        copy_out(low[:, t, at:at + m], t_, ps[t_.bank][:, 0:m])
                act.wait_ge(low_sq, 4 * (l + 1))
                for w, name in enumerate("qk"):
                    for t in range(NT):
                        t_ = tile[name, l, t]
                        full(t_)
                        last = act.activation(sq[w][:, t * WIDTH:(t + 1) * WIDTH], ps[t_.bank][:, :], ACT.Square)
                        if t == NT - 1:
                            last.then_inc(sq_ready, 1)
                        copy_out(qk_a[:, w, t, :], t_, ps[t_.bank][:, :])
                for t in range(NT):
                    t_ = tile["v", l, t]
                    full(t_)
                    copy_out(v[:, 0, t, :], t_, ps[t_.bank][:, :])
                for j, rs in enumerate(((0, 1), (2,), (3, 4))):
                    t_ = tile["lowT", l, j]
                    full(t_)
                    for n, r in enumerate(rs):
                        g = gain(l, "cq", r) if r < 3 else gain(l, "ckv", r - 3)
                        act.mul(lowT[:, r, :], ps[t_.bank][:, n * T:(n + 1) * T], g).then_inc(drained[t_.bank], 1)
                act.wait_ge(sq_used, 4 * l + 1)
                n = HEADS * B_DIM // 2
                for t in range(NT):
                    for half in range(2):
                        t_ = tile["uq", l, t, half]
                        full(t_)
                        at = (2 * t + half) * n
                        last = act.activation(sq[0][:, at:at + n], ps[t_.bank][:, 0:n], ACT.Square)
                        if t + half == 2:
                            last.then_inc(sq_ready, 1)
                        copy_out(qk_b[:, 0, t, half * n:(half + 1) * n], t_, ps[t_.bank][:, 0:n])
                for t in range(NT):
                    for half in range(2):
                        t_ = tile["ukv", l, t, half]
                        full(t_)
                        src = ps[t_.bank][:, :].rearrange("p (h c) -> p h c", h=4)
                        dst = qk_b[:, 1, t, half * n:(half + 1) * n].rearrange("p (h c) -> p h c", h=4)
                        copy_out(dst[:, :, 0:B_NOPE], t_, src[:, :, 0:B_NOPE])
                        copy_out(v[:, 1, t, half * 4 * B_V:(half + 1) * 4 * B_V].rearrange("p (h c) -> p h c", h=4), t_,
                                 src[:, :, B_NOPE:])
                act.wait_ge(kr_placed, l + 1)
                for t in range(NT):
                    for half in range(2):
                        t_ = tile["ukv", l, t, half]
                        act.wait_ge(drained[t_.bank], t_.done)
                act.wait_ge(sq_used, 4 * l + 2)
                for t in range(NT):
                    last = act.activation(sq[1][:, t * 2 * n:(t + 1) * 2 * n], qk_b[:, 1, t, :], ACT.Square)
                last.then_inc(sq_ready, 1)
                for hp in range(4):
                    t_ = tile["aT", l, hp]
                    full(t_)
                    copy_out(qkT_a[:, hp, :], t_, ps[t_.bank][:, :])

                def exponentials(k):
                    act.wait_ge(max_ready, 16 * l + k + 1)
                    b, hd = k // HEADS, k % HEADS
                    for t, (lo, hi) in enumerate(((0, P), (P, 3 * P))):
                        last = act.activation(pr[:, k % 2, lo:hi], sc[:, k % 2, lo:hi], ACT.Exp,
                                              bias=neg_max[:, k % 2, t:t + 1], accum_out=row_sum[:, b, t, hd:hd + 1])
                    last.then_inc(exp_done, 1)

                exponentials(0)
                for k in range(16):
                    t_ = tile["pT", l, k]
                    full(t_)
                    if k >= 2:
                        used_values(l, k - 2)
                    copy_out(pT[:, k % 2, :], t_, ps[t_.bank][:, 0:3 * P])
                    if k + 1 < 16:
                        exponentials(k + 1)
                    if k % 2:
                        g = k // 2
                        t_ = tile["gate", l, g]
                        full(t_)
                        if g == 0:
                            act.wait_ge(sq_used, 4 * l + 4)
                        copy_out(gate[:, 2 * g:2 * g + 2, :], t_, view(t_.bank, 2, T))
                    if k in (6, 7):
                        for hd in range(4 * (k - 6), 4 * (k - 6) + 4):
                            t_ = tile["bT", l, hd]
                            full(t_)
                            copy_out(qkT_b[0:B_DIM, hd, :], t_, ps[t_.bank][0:B_DIM, :])
                    if k == 10:
                        turned_y(l, 0)
                turned_y(l, 1)
                for g in range(8):
                    t_ = tile["gate", l, g]
                    act.wait_ge(drained[t_.bank], t_.done)
                both = gate.rearrange("p (b m) c -> p b (m c)", b=2)
                for j in range(4):
                    part_ = both[:, :, j * 2 * T:(j + 1) * 2 * T]
                    act.activation(part_, part_, ACT.Sigmoid).then_inc(gate_ready, 1)
                for t in range(NT):
                    for half in range(2):
                        t_ = tile["wo", l, t, half]
                        act.wait_ge(drained[t_.bank], t_.done)
                norm(2 * l + 1, l, "ffn", l == 0)

            def used_values(l, k):
                if k % 4 == 3:
                    t_ = tile["y", l, k // 4]
                    act.wait_ge(filled[t_.bank], t_.fill)
                else:
                    act.wait_ge(pv_done, 12 * l + k - k // 4 + 1)

            def turned_y(l, b):
                for j in range(2):
                    t_ = tile["yT", l, b, j]
                    full(t_)
                    copy_out(yT[:, 4 * b + 2 * j:4 * b + 2 * j + 2, :], t_, view(t_.bank, 2, T))

            def copy_high(q, slot, before, load):
                if load:
                    act.wait_ge(*load)
                if before is not None:
                    act.wait_ge(unit_used, before + 1)
                act.copy(w_hi[q][:, :], ring[slot][:, q * UNIT:(q + 1) * UNIT]).then_inc(hi_ready, 1)

            def silu(tiles, used):
                act.wait_ge(unit_used, used)
                for t, t_ in enumerate(tiles):
                    act.activation(sg[:, t, :], ps[t_.bank][:, 0:GROUP], ACT.Silu).then_inc(silu_done, 1)

            def turned_high(t_, tiles):
                full(t_)
                act.copy(hffT[0][:, :, 0:tiles * P], view(t_.bank, 2, T)[:, :, 0:tiles * P]).then_inc(turned_hi, 1)

            def dense():
                def up(j, s, q, turn):
                    before = None if isinstance(j, int) and j == 0 else gu_at(j - 1) + q
                    load = (loaded[DENSE_SLOTS[s]], turn * 32 + (dense_loads[s] + 32))
                    copy_high(q, DENSE_SLOTS[s], before, load if q == 0 else None)

                def down(j, s, turn):
                    for q in (4, 5):
                        load = (loaded_down[DENSE_SLOTS[s]], turn * 16 + 16)
                        copy_high(q, DENSE_SLOTS[s], dn_at(j - 1) + (q - 4), load if q == 4 else None)

                def step(j, s, turn, first=False, last=False):
                    if not first:
                        down(j - 1, 1 - s, turn)
                    if not last:
                        for q in range(3):
                            up(j + 1, 1 - s, q, turn + 1 if not first else 0)
                    silu([t_.at(j, 1, 1) for t_ in DENSE_GU], gu_at(j) + 4)
                    if not last:
                        up(j + 1, 1 - s, 3, turn)
                    turned_high(DENSE_TURN.at(j, 1, 1), NT)

                for q in range(4):
                    up(0, 0, q, 0)
                step(0, 0, 0, first=True)
                with act.Fori(0, (NGROUP - 3) // 2) as i:
                    step(i * 2 + 1, 1, i)
                    step(i * 2 + 2, 0, i)
                step(NGROUP - 2, 1, (NGROUP - 3) // 2)
                step(NGROUP - 1, 0, (NGROUP - 3) // 2, last=True)
                down(NGROUP - 1, 0, NGROUP // 2)

            act.wait_ge(x_in, 16)
            act.wait_ge(gain_in, 16 * GAIN_ROW_DMAS)
            act.wait_ge(const_in, 16)
            act.wait_ge(route_in, 16 * 5)
            act.wait_ge(gcol_set, 2)
            mixer(0)
            dense()
            for t in range(NT):
                for half in range(2):
                    t_ = tile["dense", t, half]
                    act.wait_ge(drained[t_.bank], t_.done)
            mixer(1)
            act.dma_start(g_row, a["ffn_norm"][DEPTH - 1].partition_broadcast(P)).then_inc(g_row_in, 16)
            act.wait_ge(route_ready, 1)
            act.activation(r16[4], r16[1], ACT.Exp).then_inc(route_exp, 1)

            def gathered(tiles):
                for g, t_ in enumerate(tiles):
                    full(t_)
                    act.copy(hT_parts[0][:, 4 * g:4 * g + 4, 0:CAP], view(t_.bank, 4, CAP)).then_inc(gathered_hi, 1)

            def results(i):
                act.wait_ge(unit_used, (i + 1) * UNITS)
                for half, t_ in enumerate(prev_y(i)):
                    act.copy(ye[0][:, half * 512:(half + 1) * 512], ps[t_.bank][:, :]).then_inc(ye_hi, 1)

            def take_rows(i):
                for n in range(4):
                    full(item_tile(i, "scatter", n))
                t_ = prev_selT(i)
                full(t_)
                copy_out(selT[:, :], t_, ps[t_.bank][:, 0:T])

            def expert(i):
                n = (i + 1) * UNITS

                def up(j, q):
                    slot = EXP_SLOTS[j]
                    before = i * UNITS + (gu_at(NGROUP - 1) + q) if j == 0 else n + (gu_at(j - 1) + q)
                    use = EXP_SLOTS[:j + 1].count(slot)
                    load = (loaded[slot], i * (32 * EXP_USES[slot]) + (exp_loads[slot] + 32 * use))
                    copy_high(q, slot, before, load if q == 0 else None)

                def down(j):
                    slot = EXP_SLOTS[j]
                    for q in (4, 5):
                        before = i * UNITS + (UNITS - 6 + q) if j == 0 else n + (dn_at(j - 1) + q - 4)
                        use = EXP_SLOTS[:j + 1].count(slot)
                        load = (loaded_down[slot], i * (16 * EXP_USES[slot]) + (DENSE_DOWNS[slot] + 16 * use))
                        copy_high(q, slot, before, load if q == 4 else None)

                up(0, 0)
                gathered(own_gather(i))
                for q in range(1, 4):
                    up(0, q)
                results(i)
                for j in range(NGROUP):
                    if j:
                        down(j - 1)
                    if j < NGROUP - 1:
                        for q in range(3):
                            up(j + 1, q)
                    silu([item_tile(i, "gu", j)], n + (gu_at(j) + 4))
                    if j < NGROUP - 1:
                        up(j + 1, 3)
                    if j == 1:
                        take_rows(i)
                    turned_high(item_tile(i, "turn", j), 1)
                down(NGROUP - 1)

            with act.Fori(0, NEXP) as i:
                expert(i)
            act.wait_ge(items_known, 1)
            n = act.value_load(n_items[0:1, 0:1], min_val=NEXP, max_val=ITEMS)
            with act.If(n > NEXP):
                with act.Fori(NEXP, ITEMS) as i:
                    expert(i)
            results(n)

        @block.vector
        def _(dve):
            steps = [0]

            def step(ins):
                steps[0] += 1
                ins.then_inc(dve_step, 1)
                dve.wait_ge(dve_step, steps[0])

            def full(t_):
                dve.wait_ge(filled[t_.bank], t_.fill)

            def norm(n, l, gain_name, parts=False):
                dve.wait_ge(norm_rstd, n + 1)
                for t in range(NT):
                    dve.tensor_scalar(h[:, t, :], x[:, t, :], rs_x[:, t:t + 1], None, ALU.mult).then_inc(h_scaled, 1)
                if parts:
                    for dp in range(DT // 2):
                        t_ = tile["hT", n, dp]
                        dve.wait_ge(gathered_hi, 2 * dp + 2)
                        for j in range(2):
                            m = 2 * dp + j
                            dve.scalar_tensor_tensor(
                                out=hT_parts[1][:, m, :], in0=view(t_.bank, 2, T)[:, j, :], scalar=gain(l, gain_name, m),
                                in1=hT_parts[0][:, m, :].bitcast(F32), op0=ALU.mult, op1=ALU.subtract).then_inc(
                                drained[t_.bank], 1)
                    return
                for dp in range(0, DT // 2, 2):
                    t_ = tile["hT", n, dp]
                    full(t_)
                    for j in range(2):
                        dve.tensor_scalar(hT[:, 2 * dp + j, :], view(t_.bank, 2, T)[:, j, :],
                                          gain(l, gain_name, 2 * dp + j), None, ALU.mult).then_inc(drained[t_.bank], 1)

            def head_pieces(l, w):
                branch_b = w >= 2
                buf = (qk_b if branch_b else qk_a)[:, w % 2, :, :]
                dim, rot = (B_DIM, B_ROT) if branch_b else (A_DIM, A_ROT)
                lo = B_NOPE if branch_b else 0
                name = "b" if branch_b else "a"
                heads = buf.rearrange("p t (h c) -> p (t h) c", c=dim)
                g0 = (0, A_DIM, 2 * A_DIM, 2 * A_DIM + B_DIM)[w]
                g = g_heads[:, l, g0:g0 + dim].unsqueeze(1).broadcast_to([P, NT * HEADS, dim])
                rs = rs_h[:, w, :].unsqueeze(2).broadcast_to([P, NT * HEADS, dim])
                by_head = buf.rearrange("p t (h c) -> p t h c", c=dim)
                half = rot // 2
                table = lambda s: con(f"{s}_{name}").rearrange("p (t r) -> p t r", t=NT)
                cos = table("cos").unsqueeze(2).broadcast_to([P, NT, HEADS, rot])
                sin = table("sin").unsqueeze(2).broadcast_to([P, NT, HEADS, rot])
                tmp = rot_tmp[:, 0:NT * HEADS * rot].rearrange("p (t h r) -> p t h r", t=NT, h=HEADS)
                x12 = by_head[:, :, :, lo:lo + rot]

                def scale():
                    dve.wait_ge(head_rstd, 4 * l + w + 1)
                    step(dve.tensor_tensor(heads, heads, rs, ALU.mult))

                def gains():
                    step(dve.tensor_tensor(heads, heads, g, ALU.mult))

                def cross():
                    dve.tensor_tensor(tmp[:, :, :, 0:half], x12[:, :, :, half:], sin[:, :, :, 0:half], ALU.mult)
                    step(dve.tensor_tensor(tmp[:, :, :, half:], x12[:, :, :, 0:half], sin[:, :, :, half:], ALU.mult))

                def straight():
                    step(dve.tensor_tensor(x12, x12, cos, ALU.mult))

                def total():
                    step(dve.tensor_tensor(x12, x12, tmp, ALU.add))
                    dve.sem_inc(qk_normed, 1)

                return [scale, gains, cross, straight, total]

            def mixer(l):
                norm(2 * l, l, "attn")
                dve.wait_ge(low_rstd, l + 1)
                for t in range(NT):
                    for j, (lo, hi) in enumerate(((0, Q_RANK), (Q_RANK, Q_RANK + KV_RANK))):
                        t_ = tile[("cq", "ckv")[j], l, t]
                        dve.wait_ge(drained[t_.bank], t_.done)
                        dve.tensor_scalar(low[:, t, lo:hi], low[:, t, lo:hi], rs_low[:, 2 * t + j:2 * t + j + 1], None,
                                          ALU.mult).then_inc(low_scaled, 1)

                def sum_squares(w):
                    dve.wait_ge(sq_ready, 4 * l + w + 1)
                    dim = B_DIM if w >= 2 else A_DIM
                    dve.reduce_sum(ss_h[:, w, :], sq[w % 2][:, 0:NT * HEADS * dim].rearrange("p (h c) -> p h c", c=dim),
                                   AX_X).then_inc(sq_used, 1)

                for w in range(2):
                    sum_squares(w)
                    for t in range(NT):
                        t_ = tile["qk"[w], l, t]
                        dve.wait_ge(drained[t_.bank], t_.done)
                    for piece in head_pieces(l, w):
                        piece()
                sum_squares(2)
                sum_squares(3)
                for t in range(NT):
                    for half in range(2):
                        t_ = tile["uq", l, t, half]
                        dve.wait_ge(drained[t_.bank], t_.done)

                def softmax_max(k):
                    t_ = tile["s", l, k]
                    full(t_)
                    if k >= 2:
                        dve.wait_ge(exp_done, 16 * l + k - 1)
                    scale = (A_DIM if k < HEADS else B_DIM) ** -0.5
                    ins = dve.scalar_tensor_tensor(out=sc[:, k % 2, :], in0=ps[t_.bank][:, 0:3 * P], scalar=scale,
                                                   in1=con("mask"), op0=ALU.mult, op1=ALU.add)
                    ins.then_inc(drained[t_.bank], 1)
                    dve.wait_ge(drained[t_.bank], t_.done)
                    dve.reduce_max(row_max[:, k % 2, 0:1], sc[:, k % 2, 0:P], AX_X)
                    step(dve.reduce_max(row_max[:, k % 2, 1:2], sc[:, k % 2, P:3 * P], AX_X))
                    dve.tensor_scalar(neg_max[:, k % 2, :], row_max[:, k % 2, :], -1.0, None, ALU.mult).then_inc(max_ready, 1)

                def take_y(quad):
                    b, q = quad // 2, quad % 2
                    dve.wait_ge(exp_done, 16 * l + 4 * quad + 4)
                    inv = row_inv[:, b, :, 4 * q:4 * q + 4]
                    step(dve.reciprocal(inv, row_sum[:, b, :, 4 * q:4 * q + 4]))
                    t_ = tile["y", l, quad]
                    full(t_)
                    dve.tensor_tensor(y[:, b, :, q * T:(q + 1) * T].rearrange("p t (h c) -> p t h c", c=A_DIM),
                                      ps[t_.bank][:, :].rearrange("p (t h c) -> p t h c", t=NT, c=A_DIM),
                                      inv.unsqueeze(3).broadcast_to([P, NT, 4, A_DIM]), ALU.mult).then_inc(drained[t_.bank], 1)

                pieces = head_pieces(l, 2) + head_pieces(l, 3)
                for k in range(16):
                    softmax_max(k)
                    for piece in pieces[2 * k:2 * k + 2]:
                        piece()
                    if k >= 5 and (k - 5) % 4 == 0:
                        take_y((k - 5) // 4)
                take_y(3)
                for m in range(DT):
                    t_ = tile["br", l, m]
                    full(t_)
                    dve.wait_ge(gate_ready, 4 * l + m // 2 + 1)
                    pair = prod[:, m % 2, :].rearrange("p (b c) -> p b c", b=2)
                    gates = gate.rearrange("p (b m) c -> p m b c", b=2)[:, m, :, :]
                    ins = dve.tensor_tensor(pair, view(t_.bank, 2, T), gates, ALU.mult)
                    ins.then_inc(drained[t_.bank], 1)
                    dve.wait_ge(drained[t_.bank], t_.done)
                    dve.tensor_tensor(merged[:, m, :], pair[:, 0, :], pair[:, 1, :], ALU.add).then_inc(merged_ready, 1)
                add_to_x("wo", l)
                norm(2 * l + 1, l, "ffn", l == 0)

            def add_to_x(*key):
                for t in range(NT):
                    for half in range(2):
                        t_ = tile[(*key, t, half)]
                        if key[0] != "dense":
                            full(t_)
                        xs = x[:, t, half * 512:(half + 1) * 512]
                        dve.tensor_tensor(xs, xs, ps[t_.bank][:, :], ALU.add).then_inc(drained[t_.bank], 1)

            def split_low(q, slot, n, at):
                dve.wait_ge(hi_ready, n + (at + 1))
                dve.tensor_tensor(w_lo[q][:, :], ring[slot][:, q * UNIT:(q + 1) * UNIT], w_hi[q][:, :].bitcast(F32),
                                  ALU.subtract).then_inc(split_ready, 1)

            def hidden(tiles, n_silu):
                for t, t_ in enumerate(tiles):
                    dve.wait_ge(silu_done, n_silu + t)
                    dve.tensor_tensor(hff[:, t, :], sg[:, t, :], ps[t_.bank][:, GROUP:2 * GROUP], ALU.mult).then_inc(
                        drained[t_.bank], 1)

            def turned_low(t_, n_turned, tiles):
                dve.wait_ge(turned_hi, n_turned)
                cols = slice(0, tiles * P)
                dve.tensor_tensor(hffT[1][:, :, cols], view(t_.bank, 2, T)[:, :, cols], hffT[0][:, :, cols].bitcast(F32),
                                  ALU.subtract).then_inc(drained[t_.bank], 1)

            def dense():
                def up(j, s, q):
                    split_low(q, DENSE_SLOTS[s], 0, gu_at(j) + q)

                def down(j, s):
                    for q in (4, 5):
                        split_low(q, DENSE_SLOTS[s], 0, dn_at(j) + (q - 4))

                def step(j, s, first=False):
                    if not first:
                        down(j - 1, 1 - s)
                    if not (isinstance(j, int) and j == NGROUP - 1):
                        for q in range(3):
                            up(j + 1, 1 - s, q)
                    hidden([t_.at(j, 1, 1) for t_ in DENSE_GU], j * NT + 1)
                    if not (isinstance(j, int) and j == NGROUP - 1):
                        up(j + 1, 1 - s, 3)
                    turned_low(DENSE_TURN.at(j, 1, 1), j + 1, NT)

                dve.memset(zero[:, :].bitcast(F32), 0.0).then_inc(zero_set, 1)
                for q in range(4):
                    up(0, 0, q)
                step(0, 0, True)
                with dve.Fori(0, (NGROUP - 3) // 2) as i:
                    step(i * 2 + 1, 1)
                    step(i * 2 + 2, 0)
                step(NGROUP - 2, 1)
                step(NGROUP - 1, 0)
                down(NGROUP - 1, 0)

            dve.wait_ge(x_in, 16)
            dve.wait_ge(const_in, 16)
            dve.wait_ge(route_in, 16 * 5)
            dve.wait_ge(gcol_set, 1)
            dve.tensor_copy(gcol[:, :], ps[7][:, 0:2 * GL]).then_inc(gcol_set, 1)
            dve.wait_ge(gcol_set, 2)
            mixer(0)
            dense()
            dve.wait_ge(unit_used, UNITS)
            add_to_x("dense")
            mixer(1)

            t_ = tile["route"]
            full(t_)
            dve.memset(selT[:, :].bitcast(F32), 0.0)
            dve.memset(zero[:, :].bitcast(F32), 0.0)
            dve.memset(route[:, 0:2, 0:1], -1.0)
            dve.memset(route[:, 2:4, 0:1], 0.0)
            dve.memset(route[:, 0:2, ITEMS + 1:ITEMS + 2], -1.0)
            dve.memset(route[:, 2:4, ITEMS + 1:ITEMS + 2], 0.0).then_inc(moe_zeroed, 1)
            lg, less, tmp16, chosen, ex = r16[0], r16[1], r16[2], r16[3], r16[4]
            dve.tensor_copy(lg, view(t_.bank, NT, NEXP)).then_inc(drained[t_.bank], 1)
            dve.wait_ge(drained[t_.bank], t_.done)
            other = lg.unsqueeze(2).broadcast_to([P, NT, NEXP, NEXP])
            own = lg.unsqueeze(3).broadcast_to([P, NT, NEXP, NEXP])
            lower = con("lower8").rearrange("p (e j) -> p e j", e=NEXP).unsqueeze(1).broadcast_to([P, NT, NEXP, NEXP])
            dve.tensor_tensor(r128[0], other, own, ALU.is_gt)
            step(dve.tensor_tensor(r128[1], other, own, ALU.is_equal))
            step(dve.tensor_tensor(r128[1], r128[1], lower, ALU.mult))
            step(dve.tensor_tensor(r128[0], r128[0], r128[1], ALU.add))
            step(dve.reduce_sum(tmp16, r128[0], AX_X))
            dve.tensor_scalar(chosen, tmp16, TOPK - 0.5, None, ALU.is_lt).then_inc(sel_bits, 1)
            step(dve.reduce_max(r2[0], lg, AX_X))
            dve.tensor_tensor(less, lg, r2[0].unsqueeze(2).broadcast_to([P, NT, NEXP]), ALU.subtract).then_inc(route_ready, 1)
            dve.wait_ge(sel_bits, 1)
            dve.wait_ge(route_exp, 1)
            step(dve.tensor_tensor(ex, ex, chosen, ALU.mult))
            step(dve.reduce_sum(r2[1], ex, AX_X))
            step(dve.reciprocal(r2[2], r2[1]))
            step(dve.tensor_tensor(ex, ex, r2[2].unsqueeze(2).broadcast_to([P, NT, NEXP]), ALU.mult))
            t_ = tile["rank"]
            full(t_)
            pos = ps[t_.bank][:, 0:16].rearrange("p (t e) -> p t e", t=NT)
            dve.scalar_tensor_tensor(out=tmp16, in0=pos, scalar=1.0, in1=chosen, op0=ALU.add, op1=ALU.mult)
            step(dve.reduce_max(r2[3][:, 0:1], ps[t_.bank][:, 16:24], AX_X))
            step(dve.tensor_scalar(r2[4][:, 0:1], r2[3][:, 0:1], float(CAP), float(ITEMS - NEXP), ALU.is_gt, ALU.mult))
            step(dve.tensor_scalar(r2[5][:, 0:1], r2[4][:, 0:1], float(NEXP), None, ALU.add))
            dve.tensor_copy(n_items[0:1, 0:1], r2[5][0:1, 0:1]).then_inc(items_known, 1)
            for k in range(PASSES):
                lo = 1 + k * NEXP
                dve.tensor_scalar(route[:, 0:2, lo:lo + NEXP], tmp16, -1.0 - k * CAP, None, ALU.add)
                last = dve.tensor_copy(route[:, 2:4, lo:lo + NEXP], ex)
            step(last)
            dve.sem_inc(drained[t_.bank], 1)
            slot_no = con("slot_no")

            def stage_item(staged_, column, n_staged):
                dve.tensor_copy(staged_, route[:, :, bass.ds(column, 1)].rearrange("p q i -> p (q i)")).then_inc(staged, 1)
                dve.wait_ge(staged, n_staged)

            def one_hot(column, n_staged):
                stage_item(stage, column, n_staged)
                for t in range(NT):
                    last = dve.tensor_scalar(sel[:, t, :], slot_no, stage[:, t:t + 1], None, ALU.is_equal)
                last.then_inc(sel_ready, 1)

            def gathered(tiles, n_hi):
                for g, t_ in enumerate(tiles):
                    dve.wait_ge(gathered_hi, n_hi + g)
                    cols = slice(4 * g, 4 * g + 4)
                    dve.tensor_tensor(hT_parts[1][:, cols, 0:CAP], view(t_.bank, 4, CAP),
                                      hT_parts[0][:, cols, 0:CAP].bitcast(F32), ALU.subtract).then_inc(drained[t_.bank], 1)

            one_hot(1, 1)
            dve.wait_ge(g_row_in, 16)
            for t in range(NT):
                dve.tensor_tensor(h[:, t, :], h[:, t, :], g_row, ALU.mult).then_inc(h_gained, 1)

            def results(i):
                for half, t_ in enumerate(prev_y(i)):
                    dve.wait_ge(ye_hi, i * 2 + (half + 1))
                    cols = slice(half * 512, (half + 1) * 512)
                    dve.tensor_tensor(ye[1][:, cols], ps[t_.bank][:, :], ye[0][:, cols].bitcast(F32),
                                      ALU.subtract).then_inc(drained[t_.bank], 1)

            def add_scatter(i):
                stage_item(stage_g, i, i * 2 + 2)
                for n in range(4):
                    t_ = item_tile(i, "scatter", n)
                    full(t_)
                    t, half = n // 2, n % 2
                    xs = x[:, t, half * 512:(half + 1) * 512]
                    dve.scalar_tensor_tensor(out=xs, in0=ps[t_.bank][:, :], scalar=stage_g[:, 2 + t:3 + t], in1=xs,
                                             op0=ALU.mult, op1=ALU.add).then_inc(drained[t_.bank], 1)

            def expert(i):
                n = (i + 1) * UNITS
                silus = i * NGROUP + (NT * NGROUP + 1)

                def up(j, q):
                    split_low(q, EXP_SLOTS[j], n, gu_at(j) + q)

                def down(j):
                    for q in (4, 5):
                        split_low(q, EXP_SLOTS[j], n, dn_at(j) + q - 4)

                up(0, 0)
                gathered(own_gather(i), i * 2 + (DT + 1))
                for q in range(1, 4):
                    up(0, q)
                results(i)
                for j in range(NGROUP):
                    if j:
                        down(j - 1)
                    if j < NGROUP - 1:
                        for q in range(3):
                            up(j + 1, q)
                    hidden([item_tile(i, "gu", j)], silus + j)
                    if j < NGROUP - 1:
                        up(j + 1, 3)
                    if j == 1:
                        add_scatter(i)
                    turned_low(item_tile(i, "turn", j), i * NGROUP + (NGROUP + 1 + j), 1)
                    if j == NGROUP // 2:
                        one_hot(i + 2, i * 2 + 3)
                down(NGROUP - 1)

            with dve.Fori(0, NEXP) as i:
                expert(i)
            n = dve.value_load(n_items[0:1, 0:1], min_val=NEXP, max_val=ITEMS)
            with dve.If(n > NEXP):
                with dve.Fori(NEXP, ITEMS) as i:
                    expert(i)
            for t_ in own_gather(n):
                full(t_)
                dve.sem_inc(drained[t_.bank], 1)
            results(n)
            add_scatter(n)

        @block.gpsimd
        def _(pool):
            pool.memset(half_neg[:, :], -0.5).then_inc(half_set, 1)
            pool.wait_ge(half_set, 1)

            def rstd(dst, src, parts, ms_sem, n, done):
                for lo, hi, width in parts:
                    last = pool.tensor_scalar(dst[:, lo:hi], src[:, lo:hi], 1.0 / width, EPS, ALU.mult, ALU.add)
                last.then_inc(ms_sem, 1)
                pool.wait_ge(ms_sem, n)
                w = parts[-1][1]
                pool.tensor_tensor(dst[:, 0:w], dst[:, 0:w], half_neg[:, 0:w], ALU.pow).then_inc(done, 1)

            def norm(n):
                pool.wait_ge(norm_sq, 2 * n + 2)
                rstd(rs_x, ss_x, [(0, 2, D)], norm_ms, n + 1, norm_rstd)

            for l in range(DEPTH):
                norm(2 * l)
                pool.wait_ge(low_sq, 4 * (l + 1))
                rstd(rs_low, ss_low, [(0, 1, Q_RANK), (1, 2, KV_RANK), (2, 3, Q_RANK), (3, 4, KV_RANK)], low_ms, l + 1,
                     low_rstd)
                for w in range(4):
                    if w == 2:
                        for t in range(NT):
                            t_ = tile["ckv", l, t]
                            pool.wait_ge(drained[t_.bank], t_.done)
                        for t in range(NT):
                            dst = qk_b[:, 1, t, :].rearrange("p (h c) -> p h c", c=B_DIM)[:, :, B_NOPE:]
                            src = low[:, t, Q_RANK + KV_RANK:LOW].unsqueeze(1).broadcast_to([P, HEADS, B_ROT])
                            last = pool.tensor_copy(dst, src)
                        last.then_inc(kr_placed, 1)
                    pool.wait_ge(sq_used, 4 * l + w + 1)
                    rstd(rs_h[:, w, :], ss_h[:, w, :], [(0, 16, B_DIM if w >= 2 else A_DIM)], head_ms, 4 * l + w + 1,
                         head_rstd)
                norm(2 * l + 1)


_INS = ["x", "attn_norm", "w_in", "moba_q_norm", "moba_k_norm", "mla_cq_norm", "w_uq", "mla_ckv_norm", "w_ukv",
        "mla_q_norm", "mla_k_norm", "w_branch_a", "w_branch_b", "w_out", "ffn_norm", "dense_w_gate_up",
        "dense_w_down", "router_w", "expert_w_gate_up", "expert_w_down"]


def build(nc, shapes):
    args = {n: nc.dram_tensor(f"in_{n}_dram", s, F32, kind="ExternalInput").ap() for n, s in shapes.items()}
    out = nc.dram_tensor("out_dram", (1, T, D), F32, kind="ExternalOutput").ap()
    trunk(nc, args, out)


def kernel(**inputs):
    import concourse.bacc as _bacc
    from concourse.bass_utils import run_bass_kernel_spmd as _run

    nc = _bacc.Bacc("TRN2", target_bir_lowering=False, num_devices=1)
    arrays = {n: np.ascontiguousarray(inputs[n]) for n in _INS}
    arrays["consts"] = constants()
    build(nc, {n: a.shape for n, a in arrays.items()})
    r = _run(nc, [{f"in_{n}_dram": a for n, a in arrays.items()}], core_ids=[0])
    return r.results[0]["out_dram"]
```
